# Optimizing a Trainium2 kernel written in Bass

```python
import math
import jax, jax.numpy as jnp
from jax import lax
import numpy as np

D_MODEL = 1024
BATCH = 1
SEQ = 256
DEPTH = 2
DEC_BATCH = 8
DEC_SEQ = 4
PAST_LEN = 1024
PAGE_SIZE = 128

N_EVEN = (DEPTH + 1) // 2
N_ODD = DEPTH // 2
H_A = 8
D_A = 64
Q_BLOCK = 128
MIX_A = H_A * D_A
H_B = 4
DK_B = 128
DV_B = 128
CONV_W = 4
DELTA_CHUNK = 64
CONV_DIM = H_B * (2 * DK_B + DV_B)
MIX_B = H_B * DV_B
MIX_EVEN = MIX_A + MIX_B
EVEN_WIDTHS = (MIX_A, MIX_A, MIX_A, H_A, CONV_DIM, H_B, H_B, MIX_B)
EVEN_PROJ = MIX_A * 3 + H_A + CONV_DIM + 2 * H_B + MIX_B
D_C = 2 * D_MODEL
H_C = 8
GD_C = D_C // H_C
CHUNK_C = 128
N_GROUPS = 4
EXPERTS_PER_GROUP = 8
N_EXPERTS = N_GROUPS * EXPERTS_PER_GROUP
TOP_K_INNER = 2
D_EXPERT = 256
EPS = 1e-6

kernel_name = 'fox_deltanet_gmlp_hmoe_step'

def rms_norm(x, w):
    xf = x.astype(jnp.float32)
    y = xf * lax.rsqrt(jnp.mean(xf * xf, axis=-1, keepdims=True) + EPS)
    return (y * w.astype(jnp.float32)).astype(x.dtype)

def layer_norm(x, w, b):
    xf = x.astype(jnp.float32)
    mu = jnp.mean(xf, axis=-1, keepdims=True)
    xc = xf - mu
    y = xc * lax.rsqrt(jnp.mean(xc * xc, axis=-1, keepdims=True) + EPS)
    return (y * w.astype(jnp.float32) + b.astype(jnp.float32)).astype(x.dtype)

def l2_normalize(x):
    return x * lax.rsqrt(jnp.sum(x * x, axis=-1, keepdims=True) + EPS)

def split_cols(z, widths):
    out, start = [], 0
    for w in widths:
        out.append(z[..., start:start + w])
        start += w
    return out

def causal_conv(xc, w):
    L = xc.shape[1] - (CONV_W - 1)
    out = xc[:, 0:L] * w[0]
    for i in range(1, CONV_W):
        out = out + xc[:, i:i + L] * w[i]
    return out

def fox_prompt(q, k, v, logf):
    n, L, H, D = q.shape
    scale = D ** -0.5
    c = jnp.swapaxes(jnp.cumsum(logf, axis=1), 1, 2)
    kpos = jnp.arange(L)

    def block(i):
        start = i * Q_BLOCK
        qb = lax.dynamic_slice_in_dim(q, start, Q_BLOCK, axis=1)
        cq = lax.dynamic_slice_in_dim(c, start, Q_BLOCK, axis=2)
        s = jnp.einsum('nqhd,nkhd->nhqk', qb, k).astype(jnp.float32) * scale
        s = s + cq[..., :, None] - c[:, :, None, :]
        qpos = start + jnp.arange(Q_BLOCK)
        s = jnp.where(kpos[None, :] <= qpos[:, None], s, -jnp.inf)
        p = jax.nn.softmax(s, axis=-1).astype(v.dtype)
        return jnp.einsum('nhqk,nkhd->nqhd', p, v)

    out = lax.map(block, jnp.arange(L // Q_BLOCK))
    return jnp.moveaxis(out, 0, 1).reshape(n, L, H, D)

def fox_sample(q, k, v, logf, k_past, v_past, logf_past):
    n, Q, H, D = q.shape
    P = k_past.shape[1]
    scale = D ** -0.5
    c_past = jnp.cumsum(logf_past.astype(jnp.float32), axis=1)
    c_new = c_past[:, -1:] + jnp.cumsum(logf, axis=1)
    cq = jnp.swapaxes(c_new, 1, 2)
    s_past = jnp.einsum('nqhd,nkhd->nhqk', q, k_past).astype(jnp.float32) * scale
    s_past = s_past + cq[..., :, None] - jnp.swapaxes(c_past, 1, 2)[:, :, None, :]
    s_new = jnp.einsum('nqhd,nkhd->nhqk', q, k).astype(jnp.float32) * scale
    s_new = s_new + cq[..., :, None] - cq[:, :, None, :]
    causal = jnp.arange(Q)[:, None] >= jnp.arange(Q)[None, :]
    s_new = jnp.where(causal, s_new, -jnp.inf)
    p = jax.nn.softmax(jnp.concatenate([s_past, s_new], axis=-1), axis=-1)
    return (jnp.einsum('nhqk,nkhd->nqhd', p[..., :P].astype(v.dtype), v_past)
            + jnp.einsum('nhqk,nkhd->nqhd', p[..., P:].astype(v.dtype), v))

def gated_delta_chunked(q, k, v, g, beta, s0):
    n, L = q.shape[0], q.shape[1]
    C = DELTA_CHUNK
    pad = (-L) % C
    nc = (L + pad) // C

    def to_chunks(a):
        a = jnp.pad(a, [(0, 0), (0, pad)] + [(0, 0)] * (a.ndim - 2))
        a = a.reshape((n, nc, C) + a.shape[2:])
        return jnp.swapaxes(jnp.moveaxis(a, 1, 0), 2, 3)

    qc, kc, vc, gch, bc = to_chunks(q), to_chunks(k), to_chunks(v), to_chunks(g), to_chunks(beta)
    gc = jnp.cumsum(gch, axis=-1)
    idx = jnp.arange(C)
    incl = idx[:, None] >= idx[None, :]
    strict = idx[:, None] > idx[None, :]
    decay = jnp.exp(jnp.where(incl, gc[..., :, None] - gc[..., None, :], -jnp.inf))
    kb = kc * bc[..., None]
    vb = vc * bc[..., None]
    a_mat = jnp.where(strict, jnp.einsum('...id,...jd->...ij', kb, kc) * decay, 0.0)
    eye = jnp.broadcast_to(jnp.eye(C, dtype=jnp.float32), a_mat.shape)
    t_mat = lax.linalg.triangular_solve(a_mat, eye, left_side=True, lower=True, unit_diagonal=True)
    w_v = jnp.einsum('...ij,...je->...ie', t_mat, vb)
    w_k = jnp.einsum('...ij,...jd->...id', t_mat, kb * jnp.exp(gc)[..., None])
    qk = jnp.where(incl, jnp.einsum('...id,...jd->...ij', qc, kc) * decay, 0.0)
    q_dec = qc * jnp.exp(gc)[..., None]
    k_dec = kc * jnp.exp(gc[..., -1:] - gc)[..., None]
    g_last = jnp.exp(gc[..., -1])

    def step(S, xs):
        w_v_c, w_k_c, qk_c, q_dec_c, k_dec_c, gl = xs
        v_new = w_v_c - jnp.einsum('nhcd,nhde->nhce', w_k_c, S)
        o = jnp.einsum('nhcd,nhde->nhce', q_dec_c, S) + jnp.einsum('nhij,nhje->nhie', qk_c, v_new)
        S = S * gl[..., None, None] + jnp.einsum('nhcd,nhce->nhde', k_dec_c, v_new)
        return S, o

    s_final, o = lax.scan(step, s0, (w_v, w_k, qk, q_dec, k_dec, g_last))
    o = jnp.moveaxis(jnp.swapaxes(o, 2, 3), 0, 1).reshape(n, nc * C, H_B, v.shape[-1])
    return o[:, :L], s_final

def even_mixer(h, conv_prefix, s0, past, w_in, w_out, f_bias, conv_w, a_log, dt_bias, o_norm_w):
    n, L, _ = h.shape
    z = jnp.einsum('nld,dc->nlc', h, w_in)
    qa, ka, va, fa, qkv_b, a_b, b_b, g_b = split_cols(z, EVEN_WIDTHS)
    q = qa.reshape(n, L, H_A, D_A)
    k = ka.reshape(n, L, H_A, D_A)
    v = va.reshape(n, L, H_A, D_A)
    logf = jax.nn.log_sigmoid(fa.astype(jnp.float32) + f_bias.astype(jnp.float32))
    if past is None:
        o_a = fox_prompt(q, k, v, logf)
    else:
        o_a = fox_sample(q, k, v, logf, *past)
    xc = jnp.concatenate([conv_prefix.astype(qkv_b.dtype), qkv_b], axis=1)
    new_conv = xc[:, L:]
    conv = jax.nn.silu(causal_conv(xc, conv_w)).astype(jnp.float32)
    qd, kd, vd = split_cols(conv, (H_B * DK_B, H_B * DK_B, H_B * DV_B))
    qd = l2_normalize(qd.reshape(n, L, H_B, DK_B)) * (DK_B ** -0.5)
    kd = l2_normalize(kd.reshape(n, L, H_B, DK_B))
    vd = vd.reshape(n, L, H_B, DV_B)
    g = -jnp.exp(a_log.astype(jnp.float32)) * jax.nn.softplus(a_b.astype(jnp.float32) + dt_bias.astype(jnp.float32))
    beta = jax.nn.sigmoid(b_b.astype(jnp.float32))
    o_b, s_new = gated_delta_chunked(qd, kd, vd, g, beta, s0.astype(jnp.float32))
    o_b = rms_norm(o_b, o_norm_w) * jax.nn.silu(g_b.astype(jnp.float32).reshape(n, L, H_B, DV_B))
    mixed = jnp.concatenate([o_a.reshape(n, L, MIX_A), o_b.reshape(n, L, MIX_B).astype(h.dtype)], axis=-1)
    out = jnp.einsum('nlc,cd->nld', mixed, w_out)
    return out, k, v, logf, s_new, new_conv

def odd_mixer(h, w_in, ln_w, ln_b, w_s, b_s, w_out):
    n, L, _ = h.shape
    z = jax.nn.gelu(jnp.einsum('nld,dc->nlc', h, w_in), approximate=False)
    u, v = z[..., :D_C], z[..., D_C:]
    v = layer_norm(v, ln_w, ln_b)
    pad = (-L) % CHUNK_C
    nc = (L + pad) // CHUNK_C
    vb = jnp.pad(v, ((0, 0), (0, pad), (0, 0))).reshape(n, nc, CHUNK_C, H_C, GD_C)
    idx = jnp.arange(CHUNK_C)
    w_m = jnp.where(idx[:, None] >= idx[None, :], w_s, 0.0).astype(v.dtype)
    mixed = jnp.einsum('hts,ncshd->ncthd', w_m, vb) + jnp.swapaxes(b_s, 0, 1)[None, None, :, :, None]
    mixed = mixed.reshape(n, nc * CHUNK_C, D_C)[:, :L]
    out = jnp.einsum('nlc,cd->nld', u * mixed, w_out)
    return out, v

def hier_moe(h, w_rg, w_re, w_gate, w_up, w_down):
    pg_logits = jnp.einsum('nld,dg->nlg', h, w_rg).astype(jnp.float32)
    pg = jax.nn.softmax(pg_logits, axis=-1)
    g_sel = jnp.argmax(pg_logits, axis=-1)
    p_sel = jnp.take_along_axis(pg, g_sel[..., None], axis=-1)[..., 0]
    le = jnp.einsum('nld,de->nle', h, w_re).astype(jnp.float32)
    le = le.reshape(le.shape[:-1] + (N_GROUPS, EXPERTS_PER_GROUP))
    le_sel = jnp.take_along_axis(le, g_sel[..., None, None], axis=2)[..., 0, :]
    top_v, top_i = lax.top_k(le_sel, TOP_K_INNER)
    weights = p_sel[..., None] * jax.nn.softmax(top_v, axis=-1)
    expert_idx = g_sel[..., None] * EXPERTS_PER_GROUP + top_i
    gates = jnp.sum(jax.nn.one_hot(expert_idx, N_EXPERTS, dtype=jnp.float32) * weights[..., None], axis=-2)
    hg = jnp.einsum('nld,edf->nlef', h, w_gate)
    hu = jnp.einsum('nld,edf->nlef', h, w_up)
    act = jax.nn.silu(hg) * hu * gates.astype(h.dtype)[..., None]
    return jnp.einsum('nlef,efd->nld', act, w_down)

def setup_inputs(seed: int = 0) -> dict:
    key = jax.random.key(seed)
    ks = jax.random.split(key, 32)
    f32 = jnp.float32
    n_pages = PAST_LEN // PAGE_SIZE
    n_used = DEC_BATCH * n_pages
    n_pool = n_used + max(1, n_used // 4)

    def nrm(k, shape, scale):
        return jax.random.normal(k, shape, f32) * scale

    x_prompt = nrm(ks[0], (BATCH, SEQ, D_MODEL), 1.0)
    x_sample = nrm(ks[1], (DEC_BATCH, DEC_SEQ, D_MODEL), 1.0)
    cache_k = nrm(ks[2], (N_EVEN, n_pool, PAGE_SIZE, H_A, D_A), 1.0)
    cache_v = nrm(ks[3], (N_EVEN, n_pool, PAGE_SIZE, H_A, D_A), 1.0)
    cache_logf = jax.nn.log_sigmoid(nrm(ks[4], (N_EVEN, n_pool, PAGE_SIZE, H_A), 1.0) + 3.0)
    state_delta = nrm(ks[5], (N_EVEN, DEC_BATCH, H_B, DK_B, DV_B), 0.1)
    state_conv = nrm(ks[6], (N_EVEN, DEC_BATCH, CONV_W - 1, CONV_DIM), 1.0)
    page_table = jax.random.permutation(ks[7], n_pool)[:n_used].reshape(DEC_BATCH, n_pages).astype(jnp.int32)
    norm_mix = 1.0 + nrm(ks[8], (DEPTH, D_MODEL), 0.02)
    norm_ffn = 1.0 + nrm(ks[9], (DEPTH, D_MODEL), 0.02)
    norm_final = 1.0 + nrm(ks[10], (D_MODEL,), 0.02)
    w_in_even = nrm(ks[11], (N_EVEN, D_MODEL, EVEN_PROJ), D_MODEL ** -0.5)
    w_out_even = nrm(ks[12], (N_EVEN, MIX_EVEN, D_MODEL), MIX_EVEN ** -0.5)
    fox_forget_bias = jax.random.uniform(ks[13], (N_EVEN, H_A), f32, minval=1.0, maxval=4.0)
    dn_conv_w = nrm(ks[14], (N_EVEN, CONV_W, CONV_DIM), CONV_W ** -0.5)
    dn_a_log = jnp.log(jax.random.uniform(ks[15], (N_EVEN, H_B), f32, minval=1.0, maxval=16.0))
    dt = jnp.exp(jax.random.uniform(ks[16], (N_EVEN, H_B), f32, minval=math.log(1e-3), maxval=math.log(1e-1)))
    dn_dt_bias = dt + jnp.log(-jnp.expm1(-dt))
    dn_norm_w = 1.0 + nrm(ks[17], (N_EVEN, DV_B), 0.02)
    w_in_odd = nrm(ks[18], (N_ODD, D_MODEL, 2 * D_C), D_MODEL ** -0.5)
    gm_ln_w = 1.0 + nrm(ks[19], (N_ODD, D_C), 0.02)
    gm_ln_b = nrm(ks[20], (N_ODD, D_C), 0.02)
    gm_spatial_w = nrm(ks[21], (N_ODD, H_C, CHUNK_C, CHUNK_C), CHUNK_C ** -0.5)
    gm_spatial_b = 1.0 + nrm(ks[22], (N_ODD, H_C, CHUNK_C), 0.02)
    w_out_odd = nrm(ks[23], (N_ODD, D_C, D_MODEL), D_C ** -0.5)
    moe_router_group = nrm(ks[24], (DEPTH, D_MODEL, N_GROUPS), D_MODEL ** -0.5)
    moe_router_expert = nrm(ks[25], (DEPTH, D_MODEL, N_EXPERTS), D_MODEL ** -0.5)
    moe_w_gate = nrm(ks[26], (DEPTH, N_EXPERTS, D_MODEL, D_EXPERT), D_MODEL ** -0.5)
    moe_w_up = nrm(ks[27], (DEPTH, N_EXPERTS, D_MODEL, D_EXPERT), D_MODEL ** -0.5)
    moe_w_down = nrm(ks[28], (DEPTH, N_EXPERTS, D_EXPERT, D_MODEL), D_EXPERT ** -0.5)
    return {'x_prompt': x_prompt, 'x_sample': x_sample, 'cache_k': cache_k, 'cache_v': cache_v,
            'cache_logf': cache_logf, 'state_delta': state_delta, 'state_conv': state_conv,
            'page_table': page_table, 'norm_mix': norm_mix, 'norm_ffn': norm_ffn, 'norm_final': norm_final,
            'w_in_even': w_in_even, 'w_out_even': w_out_even, 'fox_forget_bias': fox_forget_bias,
            'dn_conv_w': dn_conv_w, 'dn_a_log': dn_a_log, 'dn_dt_bias': dn_dt_bias, 'dn_norm_w': dn_norm_w,
            'w_in_odd': w_in_odd, 'gm_ln_w': gm_ln_w, 'gm_ln_b': gm_ln_b, 'gm_spatial_w': gm_spatial_w,
            'gm_spatial_b': gm_spatial_b, 'w_out_odd': w_out_odd, 'moe_router_group': moe_router_group,
            'moe_router_expert': moe_router_expert, 'moe_w_gate': moe_w_gate, 'moe_w_up': moe_w_up,
            'moe_w_down': moe_w_down}

def reference(x_prompt, x_sample, cache_k, cache_v, cache_logf, state_delta, state_conv, page_table,
              norm_mix, norm_ffn, norm_final, w_in_even, w_out_even, fox_forget_bias, dn_conv_w,
              dn_a_log, dn_dt_bias, dn_norm_w, w_in_odd, gm_ln_w, gm_ln_b, gm_spatial_w, gm_spatial_b,
              w_out_odd, moe_router_group, moe_router_expert, moe_w_gate, moe_w_up, moe_w_down):
    n_p = x_prompt.shape[0]
    n_s = x_sample.shape[0]
    past_len = page_table.shape[1] * cache_k.shape[2]
    xp, xs = x_prompt, x_sample
    kp, vp, lfp, sdp, scp = [], [], [], [], []
    ksm, vsm, lfs, sds, scs = [], [], [], [], []
    chunk_v = []
    for layer in range(DEPTH):
        hp = rms_norm(xp, norm_mix[layer])
        hs = rms_norm(xs, norm_mix[layer])
        if layer % 2 == 0:
            e = layer // 2
            prm = (w_in_even[e], w_out_even[e], fox_forget_bias[e], dn_conv_w[e], dn_a_log[e],
                   dn_dt_bias[e], dn_norm_w[e])
            conv0 = jnp.zeros((n_p, CONV_W - 1, CONV_DIM), xp.dtype)
            s0 = jnp.zeros((n_p, H_B, DK_B, DV_B), jnp.float32)
            mp, k1, v1, lf1, sd1, sc1 = even_mixer(hp, conv0, s0, None, *prm)
            past = (cache_k[e, page_table].reshape(n_s, past_len, H_A, D_A),
                    cache_v[e, page_table].reshape(n_s, past_len, H_A, D_A),
                    cache_logf[e, page_table].reshape(n_s, past_len, H_A))
            ms, k2, v2, lf2, sd2, sc2 = even_mixer(hs, state_conv[e], state_delta[e], past, *prm)
            kp.append(k1); vp.append(v1); lfp.append(lf1); sdp.append(sd1); scp.append(sc1)
            ksm.append(k2); vsm.append(v2); lfs.append(lf2); sds.append(sd2); scs.append(sc2)
        else:
            o = layer // 2
            prm = (w_in_odd[o], gm_ln_w[o], gm_ln_b[o], gm_spatial_w[o], gm_spatial_b[o], w_out_odd[o])
            mp, _ = odd_mixer(hp, *prm)
            ms, v_rows = odd_mixer(hs, *prm)
            chunk_v.append(v_rows)
        xp = xp + mp
        xs = xs + ms
        mprm = (moe_router_group[layer], moe_router_expert[layer], moe_w_gate[layer], moe_w_up[layer],
                moe_w_down[layer])
        xp = xp + hier_moe(rms_norm(xp, norm_ffn[layer]), *mprm)
        xs = xs + hier_moe(rms_norm(xs, norm_ffn[layer]), *mprm)
    y_prompt = rms_norm(xp, norm_final)
    y_sample = rms_norm(xs, norm_final)
    return (y_prompt, y_sample, jnp.stack(kp), jnp.stack(vp), jnp.stack(lfp), jnp.stack(sdp), jnp.stack(scp),
            jnp.stack(ksm), jnp.stack(vsm), jnp.stack(lfs), jnp.stack(sds), jnp.stack(scs), jnp.stack(chunk_v))


_drawn_inputs = setup_inputs


def setup_inputs(seed=0):
    import zlib

    import numpy as np

    out = dict(_drawn_inputs(seed))
    spreads = {}
    factors = {'norm_final': 8.526, 'gm_ln_w': 8.554, 'gm_ln_b': 8.414}
    for name, (base, spread) in spreads.items():
        noise = np.random.default_rng([zlib.crc32(name.encode()), seed]).standard_normal(out[name].shape)
        drawn = base * np.exp(spread * noise) if base else spread * noise
        out[name] = __import__('jax').numpy.asarray(drawn.astype(out[name].dtype))
    for name, factor in factors.items():
        out[name] = (out[name] * factor).astype(out[name].dtype)
    return out
```

```python
from contextlib import ExitStack

import concourse.bass as bass
from concourse import mybir

F32 = mybir.dt.float32
I32 = mybir.dt.int32
ALU = mybir.AluOpType
ACT = mybir.ActivationFunctionType
AX = mybir.AxisListType

P = 128
D = 1024
KD = D // P
TP, NB, QS = 256, 8, 4
TS = NB * QS
T = TP + TS
TOK = [(0, 128), (128, 128), (256, TS)]
EPS = 1e-6
HA, DA = 8, 64
NPAIR = HA // 2
NPAGE, PG = 8, 128
HB, DB = 4, 128
CW = 4
NCT = 12
XC = (CW - 1) + TP + NB * (CW - 1 + QS)
XS = CW - 1 + TP
BIG = 1.0e30
NG, EG = 4, 8
NE = NG * EG
DE = 256
FT = DE // P
C = 96
ROUNDS = T // C
ITERS = ROUNDS * NG
SLOTS = 8
UNIT = 2048
EVEN_UNITS, ODD_UNITS, MOE_UNITS = 18, 24, 3 * EG
DC = 2048
NU = DC // P
HC = 8

SEMS = """x_loaded small_loaded pagetab_loaded consts ss_done rms_done h_ready hT_ps hT_done
 fz_ps fz_copied fz_abs  fz_ln fz_sig  
 proj_ps proj_done w_used kv_ps kv_copied  cs_ps cs_copied cs27 cst_ps cst_done cw_ps cw_done
  conv_raw conv_done neglogf qz_ready
 pa_s_ps pa_max pa_exp pa_p pa_pt_ps pa_pt pa_o_ps pa_o
 kpage_free vpage_free kt_ps kt_done ks_done bias_pages sa_s_ps sa_max sa_exp sa_p sa_pt_ps sa_pt sa_o_ps sa_o
 s0_loaded dl_sq dl_ss_ps dl_rms dl_qk dl_tok_ps dl_tok dl_R_ps dl_eR dl_cols_ps dl_cols dl_dt dl_dtx dl_kk_ps dl_kk
 dl_mt dl_u_ps dl_u dl_t_ps dl_t dl_scaled dl_w_ps dl_w dl_qdec dl_v1_ps dl_v1 dl_s_ps dl_s dl_vs_ps dl_vsT dl_vt_ps dl_vs
 dl_o_ps dl_o dl_osq dl_oss_ps dl_orms dl_mixed dl_vexp dl_su_ps dl_su dl_st_out
  x_new ws_loaded ws_ps ws_done wrep_ps wrep_done gm_v_ps gm_v gm_u_ps gm_u gm_sum gm_sq gm_rms gm_vn gm_bias
 gm_m_ps gm_m rl_ps  rt_e4x rt_exp2 rt_oh rank_ps rank_done flag_ready
 perm_ready hg_ps hg_done gs_ps gs_done pt_ps pt_done g_used gu_ps silu_done act_done dn_used ysb_done sc_ps xadd
 fin_y nf_loaded  out_misc dve_chain act_chain pool_chain moe_chain """.split()


class Named(dict):
    __getattr__ = dict.__getitem__


def build(nc, t):
    ctx = ExitStack()
    with ctx:
        def sb(name, shape, dt=F32):
            return ctx.enter_context(nc.sbuf_tensor(name, shape, dt))

        s = Named({n: ctx.enter_context(nc.semaphore(n)) for n in SEMS})
        s_w = [ctx.enter_context(nc.semaphore(f"w_slot{i}")) for i in range(SLOTS)]
        s_k = [ctx.enter_context(nc.semaphore(f"k_slot{i}")) for i in range(4)]
        s_v = [ctx.enter_context(nc.semaphore(f"v_slot{i}")) for i in range(4)]

        ps = ctx.enter_context(nc.psum_tensor("ps", [P, 8, 512], F32))

        x = sb("x", [P, 3, D])
        htok = sb("htok", [P, 3, D])
        hT = sb("hT", [P, KD, T])
        ring = sb("ring", [P, SLOTS, UNIT])
        work = sb("work", [P, 23700])
        cum = sb("cum", [P, 1408])
        ident = sb("ident", [P, P])
        negq = sb("negq", [P, P])
        negT = sb("negT", [P, P])
        lvl = sb("lvl", [P, 7, P])
        msk = sb("msk", [TS, 5, TS])
        iota = sb("iota", [P, 2, C])
        rev = sb("rev", [P, NE])
        nw = sb("nw", [P, 5, KD])
        sm = sb("sm", [P, 520])
        wsm = sb("wsm", [P, KD, 16])
        wr = sb("wr", [P, 2, KD, NG + NE])
        ptab = sb("ptab", [1, NB * NPAGE], I32)
        flag = sb("flag", [1, 2], I32)
        lfp = sb("lfp", [P, 2, NPAGE, 32])
        cs27 = sb("cs27", [P, NCT, 27])
        cst = sb("cst", [27, NCT * P])
        lfn = sb("lfn", [TS, P])

        ut, one = cum[:, 384:512], cum[:, 512:640]
        same, utS, negTS, negQS = (msk[:, i, :] for i in range(4))
        bsel = msk[:, 4, 0:NB]

        def col(i, n=1):
            return sm[:, i:i + n]

        ss, rms, rr, epsb = col(0, 15), col(15, 15), col(30, 15), col(45)
        biasrow, alog, expa, fz = col(46, 16), col(62, 4), col(66, 4), col(70, 48)
        fz3 = fz.rearrange("p (t c) -> p t c", t=3)
        fa = col(118, 48)
        fb = col(166, 48)
        lf = col(214, 24).rearrange("p (t h) -> p t h", t=3)
        nlf = col(238, 24).rearrange("p (t h) -> p t h", t=3)
        gg = col(262, 12).rearrange("p (t h) -> p t h", t=3)
        beta = col(274, 12).rearrange("p (t h) -> p t h", t=3)
        gcc = col(286, 12).rearrange("p (t h) -> p t h", t=3)
        egc = col(298, 12).rearrange("p (t h) -> p t h", t=3)
        kdc = col(310, 12).rearrange("p (t h) -> p t h", t=3)
        bex = col(322, 12).rearrange("p (t h) -> p t h", t=3)
        onw = col(334)
        pmax, psm, pinv = col(335, 20), col(355, 20), col(375, 20)
        cwc = col(395, 48)
        lsum, lmu, lss, lrs = col(443, 24), col(467, 3), col(470, 3), col(473, 3)
        epsq = col(476)
        fz1 = col(477, 24)

        def wk(off, *dims):
            n = 1
            for d in dims:
                n *= d
            a = work[:, off:off + n]
            if len(dims) == 2:
                return a.rearrange("p (a b) -> p a b", a=dims[0])
            if len(dims) == 3:
                return a.rearrange("p (a b c) -> p a b c", a=dims[0], b=dims[1])
            return a

        qkT = wk(0, 8, T)
        xc = wk(2304, NCT, XC)
        cv = wk(6084, NCT, T)
        gT = wk(9540, HB, T)
        A = 10692
        qz = wk(A, NB * NPAIR, P)
        kring = wk(A + 4096, 4, 512)
        kpT = wk(A + 6144, 2, NPAIR, P)
        vring = wk(A + 7168, 4, 512)
        sS = wk(A + 9216, 1056)
        sPT = wk(A + 10272, 9, P)
        pP = wk(A + 11424, 2, 384)
        pPT = wk(A + 12192, 2, 384)
        vT = wk(A + 11424, 4, T)
        craw = wk(A + 7168, NCT, XC)
        scin = wk(A + 10948, NCT * P)
        cwr = wk(A + 12484, P)
        ktok = htok[:, :, 0:512]
        vtok = htok[:, :, 512:1024]
        mixT = hT
        S0 = wk(0, NB * HB, P)
        dU = wk(A, 3, HB, P)
        dDT = dU
        dMT = wk(A + 1536, 3, HB, P)
        dT = wk(A + 3072, 3, HB, P)
        vexp = wk(A, NB, HB * P)
        dLT = wk(A + 4608, 3, HB, P)
        dQK = wk(A + 6144, 3, HB, P)
        dTT = wk(A + 7680, 3, HB, P)
        eR = wk(A + 9216, 3, HB, P)
        oT = wk(A + 10752, HB, T)
        Sp = wk(A + 11904, 2, HB, P)
        kdt = htok[:, :, 0:512].rearrange("p t (h e) -> p t h e", h=HB)
        vdt = htok[:, :, 512:1024].rearrange("p t (h e) -> p t h e", h=HB)
        kbe, vb, wkT, wv = dU, dMT, dT, dLT
        dsq = wk(A, 8, T)
        osq = wk(A + 6144, HB, T)
        vsT = wk(A + 1536, HB * TS)
        eg = wk(A + 12704, 2, P)
        lfx = wk(A + 11424, NPAGE, P)
        vrow = wk(0, 3, DC)
        uT = wk(6144, NU, T)
        lnw = wk(10752, DC)
        lnb = wk(12800, DC)
        wmT = wk(14848, HC, P)
        wsn = wk(15872, HC, P)
        sqj = wk(18496, DC)
        bsr = wk(18496 + DC, HC, T)
        wrep = wk(15872, HC * QS)
        wS = wk(15904, HC, TS)
        rep = wk(16160, NB, QS)
        M = 18496
        hg = wk(M, KD, C)
        pm = wk(M + 768, 3, C)
        pmT = wk(M + 1056, T)
        gs = wk(M + 1344, EG, C)
        sg = wk(M + 2112, 2, FT, C)
        a1 = wk(M + 2496, 2, FT, C)
        av = wk(M + 2880, 2, FT, C)
        ysb = wk(M + 3264, D)
        rt = wk(M + 4288, 3, 212)
        lg = rt[:, :, 0:36]
        d4, e4, eq4, oh4, pos = rt[:, :, 36:40], rt[:, :, 40:44], rt[:, :, 44:48], rt[:, :, 48:52], rt[:, :, 52:53]
        m4, s4, mr, v1, v2, w1, w2, ex2 = (rt[:, :, 53 + i:54 + i] for i in range(8))
        gmax = rt[0:1, 0, 75:76]
        rk, rk2 = rt[:, :, 62:66], rt[:, :, 66:70]
        pen = rt[:, :, 70:74]
        lem, eqa, oh1, oh2 = (rt[:, :, 76 + 32 * i:108 + 32 * i] for i in range(4))
        g8 = rt[:, :, 204:212]

        def bc(ap, shape):
            return ap.to_broadcast(shape)

        w_in = t["w_in_even"][0].rearrange("(p k) c -> p k c", k=KD)
        w_oe = t["w_out_even"][0].rearrange("(c p) d -> p c d", p=P)
        w_io = t["w_in_odd"][0].rearrange("(p k) c -> p k c", k=KD)
        w_oo = t["w_out_odd"][0].rearrange("(c p) d -> p c d", p=P)
        WG, WU, WD = t["moe_w_gate"], t["moe_w_up"], t["moe_w_down"]
        COLS = [1544 + c * 256 for c in range(6)] + [3088, 3344] + [c * 256 for c in range(6)]
        even_src = [w_in[:, :, c:c + 256] for c in COLS] + [w_oe[:, 2 * i:2 * i + 2, :] for i in range(4)]
        odd_src = [w_io[:, :, DC + 256 * i:DC + 256 * (i + 1)] for i in range(8)] \
            + [w_io[:, :, 256 * i:256 * (i + 1)] for i in range(8)] + [w_oo[:, 2 * i:2 * i + 2, :] for i in range(8)]

        def kview(u):
            return ring[:, u % SLOTS, :].rearrange("p (k c) -> p k c", k=KD)

        def cview(u):
            return ring[:, u % SLOTS, :].rearrange("p (c d) -> p c d", c=2)

        MOE0 = [EVEN_UNITS, EVEN_UNITS + ITERS * MOE_UNITS + ODD_UNITS]
        ODD0 = EVEN_UNITS + ITERS * MOE_UNITS

        def wait_unit(eng, u, it=0):
            eng.wait_ge(s_w[u % SLOTS], 16 * (u // SLOTS + 1) + it * (16 * MOE_UNITS // SLOTS))

        def more(eng, layer):
            eng.wait_ge(s.flag_ready, layer + 1)
            return eng.value_load(flag[0:1, layer:layer + 1], min_val=0, max_val=1)

        def skip_rounds(eng, layer, *counts):
            for sm_, per in counts:
                eng.wait_ge(sm_, (layer * ITERS + NG) * per)
                eng.sem_inc(sm_, (ITERS - NG) * per)

        block = ctx.enter_context(nc.Block())

        @block.sync
        def _(sp):
            for i, (r0, n) in enumerate(TOK):
                src = t["x_prompt"][0, r0:r0 + n, :] if i < 2 else t["x_sample"].rearrange("b q d -> (b q) d")
                sp.dma_start(x[0:n, i, :], src).then_inc(s.x_loaded, 16)

            def load(u, src, it=0):
                sp.dma_start(ring[:, u % SLOTS, :].rearrange("p (a b) -> p a b", a=src.shape[1]) if len(src.shape) == 3
                             else ring[:, u % SLOTS, :], src).then_inc(s_w[u % SLOTS], 16)

            def even_used(u):
                if u < 14:
                    sp.wait_ge(s.proj_ps, 2 * (u + 1))
                else:
                    sp.wait_ge(s.w_used, u - 13)

            def odd_used(j):
                if j < 8:
                    sp.wait_ge(s.gm_v_ps, 3 * (j + 1))
                elif j < 16:
                    sp.wait_ge(s.gm_u_ps, 2 * (j - 7))
                else:
                    sp.wait_ge(s.w_used, 4 + j - 15)

            def moe_used(layer, it, j):
                n = (it + layer * ITERS) * EG + j // 3 + 1
                sp.wait_ge((s.g_used, s.gu_ps, s.dn_used)[j % 3], n)

            def moe_load(layer, group, it, j):
                e = group * EG + j // 3
                w = (WG, WU, WD)[j % 3][layer, bass.ds(e, 1)]
                load(MOE0[layer] + j, w.rearrange("e (p k) f -> p (e k f)", p=P))

            for u in range(EVEN_UNITS):
                if u >= SLOTS:
                    even_used(u - SLOTS)
                load(u, even_src[u])
            sp.wait_ge(s.pagetab_loaded, 16)
            for grp in range(2):
                for free, landed, cache, dst in ((s.kpage_free, s_k, t["cache_k"][0], kring),
                                                 (s.vpage_free, s_v, t["cache_v"][0], vring)):
                    with sp.Fori(0, 4) as bl:
                        for pg in range(NPAGE):
                            page = sp.value_load(ptab[0:1, bass.ds(bl * NPAGE + (grp * 32 + pg), 1)], min_val=0,
                                                 max_val=cache.shape[0] - 1)
                            sp.wait_ge(free, bl * NPAGE + (grp * 32 + pg + 1))
                            sp.dma_start(dst[:, pg % 4, :], cache[bass.ds(page, 1)]
                                         .rearrange("a r h d -> r (a h d)")).then_inc(landed[pg % 4], 16)
            sp.wait_ge(s.sa_o, 4)
            sp.wait_ge(s.pa_o, HA)
            sp.dma_start(S0[:, :, :], t["state_delta"][0].rearrange("b h k v -> k (b h) v")).then_inc(s.s0_loaded, 16)
            for layer in range(2):
                for j in range(SLOTS):
                    if layer == 0:
                        even_used(EVEN_UNITS - SLOTS + j)
                    else:
                        odd_used(ODD_UNITS - SLOTS + j)
                    moe_load(layer, 0, 0, j)

                def first_groups(r):
                    with sp.Fori(0, NG - 1) as g:
                        it = g + r * NG
                        for j in range(SLOTS, MOE_UNITS + SLOTS):
                            moe_used(layer, it, j - SLOTS)
                            if j < MOE_UNITS:
                                moe_load(layer, g, it, j)
                            else:
                                moe_load(layer, g + 1, it + 1, j - MOE_UNITS)

                def last_group(r, last):
                    it = r * NG + NG - 1
                    for j in range(SLOTS, MOE_UNITS + (0 if last else SLOTS)):
                        moe_used(layer, it, j - SLOTS)
                        if j < MOE_UNITS:
                            moe_load(layer, NG - 1, it, j)
                        else:
                            moe_load(layer, 0, it + 1, j - MOE_UNITS)

                first_groups(0)
                with sp.If(more(sp, layer) > 0):
                    last_group(0, False)
                    for r in range(1, ROUNDS):
                        first_groups(r)
                        last_group(r, r == ROUNDS - 1)
                with sp.Else():
                    last_group(0, True)
                    for k in range(SLOTS):
                        u = MOE0[layer] + NG * MOE_UNITS - SLOTS + k
                        wait_unit(sp, u)
                        sp.sem_inc(s_w[u % SLOTS], 16 * (ITERS - NG) * MOE_UNITS // SLOTS)
                if layer == 0:
                    for j in range(ODD_UNITS):
                        if j < SLOTS:
                            moe_used(0, ITERS - 1, MOE_UNITS - SLOTS + j)
                        else:
                            odd_used(j - SLOTS)
                        load(ODD0 + j, odd_src[j])
            sp.wait_ge(s.fin_y, 3)
            sp.dma_start(t["y_prompt"][0, 0:P, :], htok[:, 0, :]).then_inc(s.out_misc, 16)
            sp.dma_start(t["y_prompt"][0, P:TP, :], htok[:, 1, :]).then_inc(s.out_misc, 16)
            sp.dma_start(t["y_sample"].rearrange("b q d -> (b q) d"), htok[0:TS, 2, :]).then_inc(s.out_misc, 16)
            sp.wait_ge(s.out_misc, 16 * 17)

        @block.gpsimd
        def _(pool):
            n = [0]

            def ch(ins):
                n[0] += 1
                ins.then_inc(s.pool_chain, 1)
                pool.wait_ge(s.pool_chain, n[0])

            def sel(ap, pattern, base, cm, fill=0.0, op=ALU.is_ge):
                ch(nc.gpsimd.affine_select(out=ap, in_=ap, compare_op=op, fill=fill, base=base,
                                           pattern=pattern, channel_multiplier=cm))

            pool.dma_start(ptab[:, :], t["page_table"].rearrange("(o b) n -> o (b n)", o=1)).then_inc(s.pagetab_loaded, 16)
            ch(nc.gpsimd.memset(cum[:, 0:384], 0.0))
            ch(nc.gpsimd.memset(cum[:, 384:1408], 1.0))
            sel(ut, [[1, P]], 0, -1)
            ch(nc.gpsimd.memset(ident[:, :], 0.0))
            sel(ident[:, :], [[-1, P]], 0, 1, 1.0, ALU.not_equal)
            ch(nc.gpsimd.memset(negq[:, :], 0.0))
            sel(negq[:, :], [[-1, P]], 0, 1, -BIG)
            ch(nc.gpsimd.memset(negT[:, :], 0.0))
            sel(negT[:, :], [[1, P]], 0, -1, -BIG)
            ch(nc.gpsimd.memset(lvl[:, :, :], 0.0))
            for l in range(7):
                b = 1 << l
                v = lvl[:, l, :].rearrange("p (n two b) -> p n two b", two=2, b=b)[:, :, 1, :]
                ch(nc.gpsimd.memset(v, 1.0))
                sel(v, [[-2 * b, P // (2 * b)], [0, b]], 0, 1)
                sel(v, [[2 * b, P // (2 * b)], [0, b]], b - 1, -1)
            m4d = msk[:, :, :].rearrange("p m (b q) -> p m b q", q=QS)
            ch(nc.gpsimd.memset(msk[:, 0:2, :], 1.0))
            ch(nc.gpsimd.memset(msk[:, 2:4, :], 0.0))
            ch(nc.gpsimd.memset(msk[:, 4, :], 1.0))
            for m, fill in ((0, 0.0), (1, 0.0), (2, -BIG), (3, -BIG)):
                sel(m4d[:, m], [[-QS, NB], [0, QS]], 0, 1, fill)
                sel(m4d[:, m], [[QS, NB], [0, QS]], QS - 1, -1, fill)
            sel(utS, [[1, TS]], 0, -1)
            sel(negTS, [[1, TS]], 0, -1, -BIG)
            sel(negQS, [[-1, TS]], 0, 1, -BIG)
            sel(bsel, [[-QS, NB]], 0, 1)
            sel(bsel, [[QS, NB]], QS - 1, -1)
            ch(nc.gpsimd.iota(iota[:, 0, :], pattern=[[1, C]], base=0, channel_multiplier=0,
                              allow_small_or_imprecise_dtypes=True))
            nc.gpsimd.iota(rev[:, :], pattern=[[-1, NE]], base=NE, channel_multiplier=0,
                           allow_small_or_imprecise_dtypes=True).then_inc(s.consts, 1)
            pool.wait_ge(s.pagetab_loaded, 16)
            cl = t["cache_logf"][0]
            for grp in range(2):
                with pool.Fori(0, 4) as bl:
                    for pg in range(NPAGE):
                        page = pool.value_load(ptab[0:1, bass.ds(bl * NPAGE + (grp * 32 + pg), 1)], min_val=0,
                                               max_val=cl.shape[0] - 1)
                        pool.dma_start(lfp[:, grp, pg, bass.ds(bl * 8, 8)],
                                       cl[bass.ds(page, 1)].rearrange("a r h -> r (a h)")).then_inc(s.bias_pages, 16)

        @block.tensor
        def _(pe):
            mm = nc.tensor.matmul
            tr = nc.tensor.transpose

            def transpose_h(n):
                pe.wait_ge(s.h_ready, 3 * (n + 1))
                for k in range(KD):
                    if k >= 4:
                        pe.wait_ge(s.hT_done, KD * n + k - 3)
                    for i, (r0, m) in enumerate(TOK):
                        last = tr(ps[:, k % 4, r0:r0 + m], htok[0:m, i, k::KD], ident[0:m, 0:m])
                    last.then_inc(s.hT_ps, 1)
                pe.wait_ge(s.hT_done, KD * (n + 1))

            def out_proj(u0, units, first_used):
                for j in range(units):
                    wait_unit(pe, u0 + j)
                    w = cview(u0 + j)
                    for c in range(2):
                        lhs = mixT if units == 4 else uT
                        for i, (r0, m) in enumerate(TOK):
                            for hf in range(2):
                                last = mm(ps[0:m, 2 * i + hf, :], lhs[:, 2 * j + c, r0:r0 + m],
                                          w[:, c, 512 * hf:512 * (hf + 1)],
                                          start=(j == 0 and c == 0), stop=(j == units - 1 and c == 1))
                    last.then_inc(s.w_used, 1)

            pe.wait_ge(s.consts, 1)
            transpose_h(0)
            pe.wait_ge(s.small_loaded, 16 * 16)
            for i, (r0, m) in enumerate(TOK):
                for k in range(KD):
                    last = mm(ps[0:m, 4, 16 * i:16 * i + 16], hT[:, k, r0:r0 + m], wsm[:, k, :],
                              start=k == 0, stop=k == KD - 1)
            last.then_inc(s.fz_ps, 1)
            tr(ps[:, 6, 0:48], cwr[0:48, :], ident[0:48, 0:48]).then_inc(s.cw_ps, 1)
            for c in range(NCT):
                last = tr(ps[:, 5, 24 * c:24 * (c + 1)], scin[0:24, P * c:P * (c + 1)], ident[0:24, 0:24])
            last.then_inc(s.cs_ps, 1)
            for c in range(28):
                if c % 2 == 0:
                    wait_unit(pe, c // 2)
                if c >= 4:
                    pe.wait_ge(s.proj_done, c - 3)
                w = kview(c // 2)
                for k in range(KD):
                    last = mm(ps[:, c % 4, 0:T], w[:, k, P * (c % 2):P * (c % 2 + 1)], hT[:, k, :],
                              start=k == 0, stop=k == KD - 1)
                last.then_inc(s.proj_ps, 1)
            pe.wait_ge(s.proj_done, 28)
            for j in range(6):
                i, (r0, m) = j // 2, TOK[j // 2]
                if j >= 3:
                    pe.wait_ge(s.kv_copied, j - 2)
                for c in range(4):
                    src = qkT[:, 4 + c, r0:r0 + m] if j % 2 == 0 else vT[:, c, r0:r0 + m]
                    last = tr(ps[0:m, j % 3, P * c:P * (c + 1)], src, ident[:, :])
                last.then_inc(s.kv_ps, 1)
            pe.wait_ge(s.cs27, 2)
            pe.wait_ge(s.cs_copied, 1)
            pe.wait_ge(s.cw_done, 1)
            for c in range(NCT):
                last = tr(ps[0:27, 5 + c // 4, P * (c % 4):P * (c % 4 + 1)], cs27[:, c, :], ident[:, :])
            last.then_inc(s.cst_ps, 1)
            pe.wait_ge(s.neglogf, 1)
            pe.wait_ge(s.kv_copied, 6)

            def pa_scores(h):
                pr, o = h // 2, 64 * (h % 2)
                b = ps[:, h % 2, :]
                if h >= 2:
                    pe.wait_ge(s.pa_exp, 2 * (h - 1))
                    pe.wait_ge(s.pa_max, 2 * (h - 1))
                for qb, c0, nk in ((0, 0, P), (1, P, TP)):
                    mm(b[:, c0:c0 + nk], qkT[o:o + 64, pr, P * qb:P * (qb + 1)], qkT[o:o + 64, 4 + pr, 0:nk],
                       start=True, stop=False, skip_group_check=True)
                    mm(b[:, c0:c0 + nk], bc(nlf[:, 0, h:h + 1], [P, P]), cum[:, 384:384 + nk],
                       start=False, stop=False, skip_group_check=True)
                    if qb:
                        mm(b[:, c0 + P:c0 + nk], bc(nlf[:, 1, h:h + 1], [P, P]), ut,
                           start=False, stop=False, skip_group_check=True)
                    last = mm(b[:, c0 + nk - P:c0 + nk], ident[:, :], negq[:, :], start=False, stop=True,
                              skip_group_check=True)
                last.then_inc(s.pa_s_ps, 1)

            def pa_out(h):
                pr = h // 2
                pe.wait_ge(s.pa_p, 2 * (h + 1))
                if h == 1:
                    pe.wait_ge(s.cst_done, 1)
                if h >= 2:
                    pe.wait_ge(s.pa_pt, h - 1)
                for j in range(3):
                    last = tr(ps[:, 2 + h % 2, P * j:P * (j + 1)], pP[:, h % 2, P * j:P * (j + 1)], ident[:, :])
                last.then_inc(s.pa_pt_ps, 1)
                pe.wait_ge(s.pa_pt, h + 1)
                if h >= 2:
                    pe.wait_ge(s.pa_o, h - 1)
                b = ps[:, 4 + h % 2, :]
                mm(b[:, 0:TP], vtok[:, 0, P * pr:P * (pr + 1)], pPT[:, h % 2, 0:TP], start=True, stop=False,
                   skip_group_check=True)
                mm(b[:, P:TP], vtok[:, 1, P * pr:P * (pr + 1)], pPT[:, h % 2, TP:384], start=False, stop=True,
                   skip_group_check=True).then_inc(s.pa_o_ps, 1)

            for h in range(HA + 1):
                if h < HA:
                    pa_scores(h)
                if h:
                    pa_out(h - 1)
            pe.wait_ge(s.pa_o, HA)
            pe.wait_ge(s.qz_ready, 1)

            def k_transpose(n):
                pe.wait_ge(s_k[n % 4], 16 * (n // 4 + 1))
                if n >= 2:
                    pe.wait_ge(s.kt_done, n - 1)
                for c in range(NPAIR):
                    last = tr(ps[:, 3 + n % 2, P * c:P * (c + 1)], kring[:, n % 4, P * c:P * (c + 1)], ident[:, :])
                last.then_inc(s.kt_ps, 1)

            for grp in range(2):
                pe.wait_ge(s.bias_pages, 16 * 64)
                pe.wait_ge(s.ks_done, grp + 1)
                if grp:
                    pe.wait_ge(s.sa_exp, 1)
                for pg in range(NPAGE):
                    lhs = lfx[:, pg, :]
                    if pg < 4:
                        mm(ps[:, 0, :], lhs, cum[:, 384 - P * pg:384 - P * pg + 512], start=pg == 0, stop=False,
                           skip_group_check=True)
                    o1 = 384 + 512 - P * pg
                    mm(ps[:, 1, :], lhs, cum[:, o1:o1 + 512], start=pg == 0, stop=False, skip_group_check=True)
                    mm(ps[:, 2, 0:TS], lhs, cum[:, 512:512 + TS], start=pg == 0, stop=False, skip_group_check=True)
                mm(ps[:, 2, 0:TS], lfn[0:TS, :], utS, start=False, stop=False, skip_group_check=True)
                mm(ps[:, 2, 0:TS], eg[0:TS, grp, :], negQS, start=False, stop=False, skip_group_check=True)
                k_transpose(32 * grp)
                for n in range(32 * grp, 32 * grp + 32):
                    if n < 32 * grp + 31:
                        k_transpose(n + 1)
                    b, pg = n // NPAGE, n % NPAGE
                    pe.wait_ge(s.kt_done, n + 1)
                    for c in range(NPAIR):
                        last = mm(ps[:, pg // 4, P * (pg % 4):P * (pg % 4 + 1)], qz[:, NPAIR * b + c, :],
                                  kpT[:, n % 2, c, :], start=False, stop=False, skip_group_check=True)
                    last.then_inc(s.kpage_free, 1)
                for b in range(4 * grp, 4 * grp + 4):
                    for c in range(NPAIR):
                        last = mm(ps[:, 2, 0:TS], qz[:, NPAIR * b + c, :], qkT[:, 4 + c, TP:T],
                                  start=False, stop=(b % 4 == 3 and c == 3), skip_group_check=True)
                last.then_inc(s.sa_s_ps, 1)
                pe.wait_ge(s.sa_p, grp + 1)
                if grp:
                    pe.wait_ge(s.sa_o, 2)
                for j in range(9):
                    m = P if j < 8 else TS
                    if j == 8:
                        last = tr(ps[0:TS, 7, 0:P], sS[:, 1024:1056], ident[:, :])
                    else:
                        last = tr(ps[:, 5 + j // 4, P * (j % 4):P * (j % 4 + 1)], sS[:, P * j:P * (j + 1)], ident[:, :])
                last.then_inc(s.sa_pt_ps, 1)
                pe.wait_ge(s.sa_pt, grp + 1)
                ov = ps[:, 7, 128:256].rearrange("p (b c j) -> p b c j", b=4, c=NPAIR)
                for n in range(32):
                    bl, pg = n // NPAGE, n % NPAGE
                    g = 32 * grp + n
                    pe.wait_ge(s_v[g % 4], 16 * (g // 4 + 1))
                    for c in range(NPAIR):
                        last = mm(ov[:, bl, c, :], vring[:, g % 4, P * c:P * (c + 1)],
                                  sPT[:, pg, 32 * bl + 8 * c:32 * bl + 8 * c + 8], start=(n == 0 and c == 0), stop=False,
                                  skip_group_check=True)
                    last.then_inc(s.vpage_free, 1)
                for bl in range(4):
                    for c in range(NPAIR):
                        last = mm(ov[:, bl, c, :], vtok[0:TS, 2, P * c:P * (c + 1)],
                                  sPT[0:TS, 8, 32 * bl + 8 * c:32 * bl + 8 * c + 8], start=False,
                                  stop=(bl == 3 and c == 3), skip_group_check=True)
                last.then_inc(s.sa_o_ps, 1)
            pe.wait_ge(s.dl_sq, 1)
            pe.wait_ge(s.sa_o, 4)
            for j in range(8):
                if j >= 4:
                    pe.wait_ge(s.dl_rms, j - 3)
                mm(ps[:, j % 4, 0:T], one, dsq[:, j, :], start=True, stop=True).then_inc(s.dl_ss_ps, 1)
            pe.wait_ge(s.dl_rms, 8)
            pe.wait_ge(s.dl_qk, 8)
            for j in range(6):
                i, (r0, m) = j // 2, TOK[j // 2]
                if j >= 3:
                    pe.wait_ge(s.dl_tok, j - 2)
                for c in range(4):
                    last = tr(ps[0:m, j % 3, P * c:P * (c + 1)], cv[:, (4 if j % 2 == 0 else 8) + c, r0:r0 + m],
                              ident[:, :])
                last.then_inc(s.dl_tok_ps, 1)
            for i in range(3):
                m = TOK[i][1]
                tri = ut if i < 2 else utS
                for h in range(HB):
                    last = mm(ps[:, 3 + i, P * h:P * h + m], bc(gg[0:m, i, h:h + 1], [m, P]), tri,
                              start=True, stop=True)
                last.then_inc(s.dl_R_ps, 1)
            for i in range(3):
                m = TOK[i][1]
                mm(ps[0:m, 6, 4 * i:4 * i + 4], ut if i < 2 else utS, gg[0:m, i, :], start=True, stop=True)
                last = mm(ps[0:m, 6, 16 + 4 * i:20 + 4 * i], one if i < 2 else same, gg[0:m, i, :], start=True,
                          stop=True)
            last.then_inc(s.dl_cols_ps, 1)
            pe.wait_ge(s.dl_tok, 6)
            for i, (r0, m) in enumerate(TOK):
                if i:
                    pe.wait_ge(s.dl_kk, 2 * i)
                for w in range(2):
                    for h in range(HB):
                        last = mm(ps[0:m, w, P * h:P * h + m], cv[:, 4 + h, r0:r0 + m],
                                  cv[:, (4 if w == 0 else 0) + h, r0:r0 + m], start=True, stop=True)
                last.then_inc(s.dl_kk_ps, 1)
            pe.wait_ge(s.dl_kk, 6)
            pe.wait_ge(s.dl_eR, 3)
            pe.wait_ge(s.dl_dt, 12)
            nu = 0
            for l in range(7):
                for i in ((0, 1, 2) if l < 2 else (0, 1)):
                    m = TOK[i][1]
                    nu += 1
                    pe.wait_ge(s.dl_mt, nu)
                    pe.wait_ge(s.dl_t, 1 + 2 * (nu - 1))
                    for h in range(HB):
                        last = mm(ps[0:m, 0, P * h:P * h + m], dMT[0:m, i, h, 0:m], dT[0:m, i, h, 0:m],
                                  start=True, stop=True)
                    last.then_inc(s.dl_u_ps, 1)
                    pe.wait_ge(s.dl_u, nu)
                    for h in range(HB):
                        mm(ps[0:m, 2, P * h:P * h + m], dTT[0:m, i, h, 0:m], dU[0:m, i, h, 0:m], start=True, stop=True)
                    for h in range(HB):
                        last = mm(ps[0:m, 4, P * h:P * h + m], dU[0:m, i, h, 0:m], dTT[0:m, i, h, 0:m],
                                  start=True, stop=True)
                    last.then_inc(s.dl_t_ps, 1)
            pe.wait_ge(s.dl_scaled, 2)
            pe.wait_ge(s.dl_t, 1 + 2 * nu)
            for i, (r0, m) in enumerate(TOK):
                if i:
                    pe.wait_ge(s.dl_w, 2 * i)
                for h in range(HB):
                    mm(ps[0:m, 0, P * h:P * (h + 1)], dTT[0:m, i, h, 0:m], vb[0:m, i, h, :], start=True, stop=True)
                for h in range(HB):
                    last = mm(ps[:, 1, P * h:P * h + m], kbe[0:m, i, h, :], dTT[0:m, i, h, 0:m], start=True, stop=True)
                last.then_inc(s.dl_w_ps, 1)
            pe.wait_ge(s.dl_w, 6)
            pe.wait_ge(s.dl_qdec, 1)
            for h in range(HB):
                last = mm(ps[:, 2, P * h:P * (h + 1)], kdt[:, 0, h, :], wv[:, 0, h, :], start=True, stop=True)
            last.then_inc(s.dl_s_ps, 1)
            pe.wait_ge(s.dl_s, 1)
            for h in range(HB):
                last = mm(ps[:, 3, P * h:P * (h + 1)], wkT[:, 1, h, :], Sp[:, 0, h, :], start=True, stop=True)
            last.then_inc(s.dl_v1_ps, 1)
            pe.wait_ge(s.dl_v1, 1)
            for h in range(HB):
                last = mm(ps[:, 2, P * h:P * (h + 1)], kdt[:, 1, h, :], wv[:, 1, h, :], start=True, stop=True)
            last.then_inc(s.dl_s_ps, 1)
            pe.wait_ge(s.s0_loaded, 16)
            for h in range(HB):
                for b in range(NB):
                    last = mm(ps[:, 4, TS * h + QS * b:TS * h + QS * (b + 1)], S0[:, HB * b + h, :],
                              wkT[:, 2, h, QS * b:QS * (b + 1)], start=True, stop=True)
            last.then_inc(s.dl_vs_ps, 1)
            pe.wait_ge(s.dl_vsT, 1)
            for h in range(HB):
                last = tr(ps[0:TS, 5, P * h:P * (h + 1)], vsT[:, TS * h:TS * (h + 1)], ident[:, :])
            last.then_inc(s.dl_vt_ps, 1)
            pe.wait_ge(s.dl_vs, 1)
            for h in range(HB):
                b = ps[:, 6 + h % 2, :]
                if h >= 2:
                    pe.wait_ge(s.dl_o, h - 1)
                for i, (r0, m) in enumerate(TOK):
                    mm(b[:, r0:r0 + m], wv[0:m, i, h, :], dQK[0:m, i, h, 0:m], start=(i == 0), stop=False,
                       skip_group_check=True)
                mm(b[:, P:TP], Sp[:, 0, h, :], cv[:, h, P:TP], start=False, stop=False, skip_group_check=True)
                for q in range(NB):
                    last = mm(b[:, TP + QS * q:TP + QS * (q + 1)], S0[:, HB * q + h, :],
                              cv[:, h, TP + QS * q:TP + QS * (q + 1)], start=False, stop=q == NB - 1,
                              skip_group_check=True)
                last.then_inc(s.dl_o_ps, 1)
            pe.wait_ge(s.dl_vexp, NB)
            vx = vexp.rearrange("p b (h e) -> p b h e", h=HB)
            for j in range(8):
                h, q = j // 2, j % 2
                if j >= 2:
                    pe.wait_ge(s.dl_su, j - 1)
                mm(ps[:, j % 2, :], kdt[0:TS, 2, h, :], vx[0:TS, 4 * q:4 * q + 4, h, :], start=True,
                   stop=True).then_inc(s.dl_su_ps, 1)
            pe.wait_ge(s.dl_osq, 1)
            pe.wait_ge(s.dl_st_out, 1)
            for h in range(HB):
                mm(ps[:, 2 + h, 0:T], one, osq[:, h, :], start=True, stop=True).then_inc(s.dl_oss_ps, 1)
            pe.wait_ge(s.dl_mixed, HB)
            pe.wait_ge(s.dl_su, 8)
            pe.wait_ge(s.dl_o, HB)
            out_proj(14, 4, 0)

            def moe(layer, n):
                transpose_h(n)
                for i, (r0, m) in enumerate(TOK):
                    for k in range(KD):
                        last = mm(ps[0:m, 4, 36 * i:36 * i + 36], hT[:, k, r0:r0 + m], wr[:, layer, k, :],
                                  start=k == 0, stop=k == KD - 1)
                last.then_inc(s.rl_ps, 1)
                pe.wait_ge(s.rt_oh, layer + 1)
                for i, (r0, m) in enumerate(TOK):
                    for j in range(i + 1):
                        n_ = TOK[j][1]
                        last = mm(ps[0:m, 5, 4 * i:4 * i + 4], (ut if j == i else one)[0:n_, 0:m], oh4[0:n_, j, :],
                                  start=j == 0, stop=j == i)
                for j in range(3):
                    n_ = TOK[j][1]
                    last = mm(ps[0:1, 5, 16:20], one[0:n_, 0:1], oh4[0:n_, j, :], start=j == 0, stop=j == 2)
                last.then_inc(s.rank_ps, 1)
                pe.wait_ge(s.rank_done, layer + 1)
                def iteration(li):
                    it = li + layer * ITERS
                    pe.wait_ge(s.perm_ready, 3 * it + 3)
                    for k in range(KD):
                        for i, (r0, m) in enumerate(TOK):
                            last = mm(ps[:, k // 4, C * (k % 4):C * (k % 4 + 1)], htok[:, i, k::KD], pm[:, i, :],
                                      start=i == 0, stop=i == 2)
                    last.then_inc(s.hg_ps, 1)
                    for e in range(EG):
                        for i, (r0, m) in enumerate(TOK):
                            last = mm(ps[:, 6 + e // 4, C * (e % 4):C * (e % 4 + 1)], bc(g8[:, i, e:e + 1], [P, P]),
                                      pm[:, i, :], start=i == 0, stop=i == 2)
                    last.then_inc(s.gs_ps, 1)
                    for i, (r0, m) in enumerate(TOK):
                        last = tr(ps[0:C, 4, r0:r0 + P], pm[:, i, :], ident[:, :])
                    last.then_inc(s.pt_ps, 1)
                    pe.wait_ge(s.hg_done, 2 * it + 2)

                    def down(e):
                        u = MOE0[layer] + 3 * e + 2
                        wait_unit(pe, u, li)
                        pe.wait_ge(s.act_done, it * EG + e + 1)
                        if e == 0:
                            pe.wait_ge(s.pt_done, it + 1)
                        w = cview(u)
                        for f in range(FT):
                            for hf in range(2):
                                last = mm(ps[0:C, 4 + hf, :], av[:, e % 2, f, :], w[:, f, 512 * hf:512 * (hf + 1)],
                                          start=(e == 0 and f == 0), stop=(e == EG - 1 and f == FT - 1))
                        last.then_inc(s.dn_used, 1)

                    for e in range(EG):
                        if e >= 2:
                            pe.wait_ge(s.act_done, it * EG + e - 1)
                        b = ps[:, 2 + e % 2, 0:4 * C].rearrange("p (a f c) -> p a f c", a=2, f=FT)
                        for a in range(2):
                            u = MOE0[layer] + 3 * e + a
                            wait_unit(pe, u, li)
                            w = kview(u)
                            for f in range(FT):
                                for k in range(KD):
                                    last = mm(b[:, a, f, :], w[:, k, f::FT], hg[:, k, :], start=k == 0,
                                              stop=k == KD - 1)
                            last.then_inc((s.g_used, s.gu_ps)[a], 1)
                        if e:
                            down(e - 1)
                    down(EG - 1)
                    pe.wait_ge(s.ysb_done, 2 * it + 2)
                    pe.wait_ge(s.gs_done, 2 * it + 2)
                    for j in range(6):
                        i, (r0, m) = j // 2, TOK[j // 2]
                        if j >= 4:
                            pe.wait_ge(s.xadd, it * 6 + j - 3)
                        mm(ps[0:m, (0, 1, 6, 7)[j % 4], :], pmT[0:C, r0:r0 + m], ysb[0:C, 512 * (j % 2):512 * (j % 2 + 1)],
                           start=True, stop=True).then_inc(s.sc_ps, 1)

                with pe.Fori(0, NG) as li:
                    iteration(li)
                with pe.If(more(pe, layer) > 0):
                    with pe.Fori(NG, ITERS) as li:
                        iteration(li)
                with pe.Else():
                    skip_rounds(pe, layer, (s.hg_ps, 1), (s.gs_ps, 1), (s.pt_ps, 1), (s.g_used, EG), (s.gu_ps, EG),
                                (s.dn_used, EG), (s.sc_ps, 6))
            moe(0, 1)
            pe.wait_ge(s.xadd, 6 * ITERS)
            transpose_h(2)
            for j in range(8):
                wait_unit(pe, ODD0 + j)
                w = kview(ODD0 + j)
                for i, (r0, m) in enumerate(TOK):
                    if j >= 2:
                        pe.wait_ge(s.gm_v, 3 * (j - 2) + i + 1)
                    for k in range(KD):
                        last = mm(ps[0:m, 3 * (j % 2) + i, 0:256], hT[:, k, r0:r0 + m], w[:, k, :], start=k == 0,
                                  stop=k == KD - 1)
                    last.then_inc(s.gm_v_ps, 1)
            pe.wait_ge(s.ws_loaded, 64)
            for h in range(HC):
                if h == 4:
                    pe.wait_ge(s.ws_done, 4)
                last = tr(ps[:, 6, P * (h % 4):P * (h % 4 + 1)], wsn[:, h, :], ident[:, :])
                last.then_inc(s.ws_ps, 1)
            pe.wait_ge(s.ws_done, 9)
            mm(ps[0:TS, 7, 0:HC * QS], rep[0:QS, :, :], wmT[0:QS, :, 0:QS], start=True,
               stop=True).then_inc(s.wrep_ps, 1)
            pe.wait_ge(s.gm_v, 24)
            for c in range(NU):
                u = ODD0 + 8 + c // 2
                if c % 2 == 0:
                    wait_unit(pe, u)
                if c >= 4:
                    pe.wait_ge(s.gm_u, c - 3)
                for k in range(KD):
                    last = mm(ps[:, c % 4, 0:T], kview(u)[:, k, P * (c % 2):P * (c % 2 + 1)], hT[:, k, :],
                              start=k == 0, stop=k == KD - 1)
                last.then_inc(s.gm_u_ps, 1)
            pe.wait_ge(s.gm_vn, 3)
            pe.wait_ge(s.gm_bias, 1)
            pe.wait_ge(s.wrep_done, HC)
            pe.wait_ge(s.gm_u, NU)
            for c in range(NU):
                h = c // 2
                b = ps[:, c % 4, :]
                if c >= 4:
                    pe.wait_ge(s.gm_m, c - 3)
                mm(b[:, 0:T], cum[0:1, 512:640], bsr[0:1, h, :], start=True, stop=False, skip_group_check=True)
                for i, (r0, m) in enumerate(TOK):
                    last = mm(b[:, r0:r0 + m], vrow[0:m, i, P * c:P * (c + 1)],
                              wmT[:, h, :] if i < 2 else wS[0:TS, h, :], start=False, stop=i == 2,
                              skip_group_check=True)
                last.then_inc(s.gm_m_ps, 1)
            pe.wait_ge(s.gm_m, NU)
            out_proj(ODD0 + 16, 8, 4)
            moe(1, 3)

        @block.scalar
        def _(act):
            n = [0]
            A_ = nc.scalar.activation

            def ch(ins):
                n[0] += 1
                ins.then_inc(s.act_chain, 1)
                act.wait_ge(s.act_chain, n[0])

            sl = []
            sl.append((nw[:, 0, :], t["norm_mix"][0].rearrange("(p k) -> p k", k=KD)))
            sl.append((nw[:, 1, :], t["norm_ffn"][0].rearrange("(p k) -> p k", k=KD)))
            sl.append((nw[:, 2, :], t["norm_mix"][1].rearrange("(p k) -> p k", k=KD)))
            sl.append((nw[:, 3, :], t["norm_ffn"][1].rearrange("(p k) -> p k", k=KD)))
            sl.append((wsm[:, :, 0:8], w_in[:, :, 1536:1544]))
            sl.append((wsm[:, :, 8:16], w_in[:, :, 3080:3088]))
            for l in range(2):
                sl.append((wr[:, l, :, 0:NG], t["moe_router_group"][l].rearrange("(p k) g -> p k g", k=KD)))
                sl.append((wr[:, l, :, NG:NG + NE], t["moe_router_expert"][l].rearrange("(p k) g -> p k g", k=KD)))
            sl.append((biasrow[:, 0:8], t["fox_forget_bias"][0:1, :].partition_broadcast(P)))
            sl.append((biasrow[:, 8:12], t["dn_dt_bias"][0:1, :].partition_broadcast(P)))
            sl.append((alog, t["dn_a_log"][0:1, :].partition_broadcast(P)))
            sl.append((onw, t["dn_norm_w"][0].rearrange("(p o) -> p o", o=1)))
            sl.append((cwr[0:48, :], t["dn_conv_w"][0].rearrange("w (c p) -> (w c) p", p=P)))
            sl.append((scin[0:24, :], t["state_conv"][0].rearrange("b w c -> (b w) c")))
            assert len(sl) == 16
            for dst, src in sl:
                act.dma_start(dst, src).then_inc(s.small_loaded, 16)

            def norm_stats(n_):
                for i, (r0, m) in enumerate(TOK):
                    A_(htok[0:m, i, :], x[0:m, i, :], ACT.Square,
                       accum_out=ss[0:m, 3 * n_ + i:3 * n_ + i + 1]).then_inc(s.ss_done, 1)
                act.wait_ge(s.ss_done, 3 * (n_ + 1))
                A_(rms[:, 3 * n_:3 * n_ + 3], ss[:, 3 * n_:3 * n_ + 3], ACT.Sqrt, scale=1.0 / D,
                   bias=epsb).then_inc(s.rms_done, 1)

            act.wait_ge(s.x_loaded, 48)
            act.wait_ge(s.fz_sig, 1)
            norm_stats(0)
            act.wait_ge(s.fz_abs, 1)
            ch(A_(fa, fa, ACT.Exp, scale=-1.0))
            ch(A_(expa, alog, ACT.Exp))
            ch(A_(fz1.rearrange("p (t c) -> p t c", t=3)[:, :, 0:4], fz3[:, :, 12:16], ACT.Exp, scale=-1.0))
            A_(fb, fa, ACT.Ln, bias=1.0).then_inc(s.fz_ln, 1)

            def silu_conv(c):
                act.wait_ge(s.conv_raw, c + 1)
                A_(cv[:, c, 0:TP], craw[:, c, 0:TP], ACT.Silu)
                A_(cv[:, c, TP:T].rearrange("p (b w) -> p b w", b=NB),
                   craw[:, c, XS:XS + NB * 7].rearrange("p (b w) -> p b w", b=NB)[:, :, 0:4],
                   ACT.Silu).then_inc(s.conv_done, 1)

            for c in range(28):
                act.wait_ge(s.proj_ps, c + 1)
                b = ps[:, c % 4, :]
                if c < 12:
                    A_(xc[:, c, 3:XS], b[:, 0:TP], ACT.Copy)
                    A_(xc[:, c, XS:XC].rearrange("p (b w) -> p b w", b=NB)[:, :, 3:7],
                       b[:, TP:T].rearrange("p (b w) -> p b w", b=NB), ACT.Copy).then_inc(s.proj_done, 1)
                elif c < 16:
                    A_(gT[:, c - 12, :], b[:, 0:T], ACT.Silu).then_inc(s.proj_done, 1)
                elif c < 24:
                    A_(qkT[:, c - 16, :], b[:, 0:T], ACT.Copy, scale=DA ** -0.5 if c < 20 else 1.0)\
                        .then_inc(s.proj_done, 1)
                else:
                    A_(vT[:, c - 24, :], b[:, 0:T], ACT.Copy).then_inc(s.proj_done, 1)
                if 2 <= c < 14:
                    silu_conv(c - 2)
                if c == 14:
                    act.wait_ge(s.proj_done, NCT)
                    A_(cs27[:, :, 0:24].rearrange("p c (b w) -> p c b w", b=NB),
                       xc[:, :, XS:XC].rearrange("p c (b w) -> p c b w", b=NB)[:, :, :, 4:7], ACT.Copy)\
                        .then_inc(s.cs27, 1)
                    A_(cs27[:, :, 24:27], xc[:, :, TP:TP + 3], ACT.Copy).then_inc(s.cs27, 1)
            act.wait_ge(s.kv_copied, 6)
            for i, (r0, m) in enumerate(TOK):
                for nm, src in (("k", ktok), ("v", vtok)):
                    if i < 2:
                        dst = t[nm + "_prompt"][0, 0, r0:r0 + m].rearrange("l h d -> l (h d)")
                    else:
                        dst = t[nm + "_sample"][0].rearrange("b l h d -> (b l) (h d)")
                    act.dma_start(dst, src[0:m, i, :]).then_inc(s.out_misc, 16)
            for i, (r0, m) in enumerate(TOK):
                dst = t["logf_prompt"][0, 0, r0:r0 + m] if i < 2 else t["logf_sample"][0].rearrange("b l h -> (b l) h")
                act.dma_start(dst, lf[0:m, i, :]).then_inc(s.out_misc, 16)
            for h in range(HA):
                b = ps[:, h % 2, :]
                if h >= 2:
                    act.wait_ge(s.pa_pt_ps, h - 1)
                for qb, c0, nk in ((0, 0, P), (1, P, TP)):
                    j = 2 * h + qb
                    act.wait_ge(s.pa_max, 2 * h + 2)
                    A_(pP[:, h % 2, c0:c0 + nk], b[:, c0:c0 + nk], ACT.Exp, bias=pmax[:, j:j + 1],
                       accum_out=psm[:, j:j + 1]).then_inc(s.pa_exp, 1)
                act.wait_ge(s.pa_pt_ps, h + 1)
                A_(pPT[:, h % 2, :], ps[:, 2 + h % 2, 0:384], ACT.Copy).then_inc(s.pa_pt, 1)
            act.wait_ge(s.cst_done, 1)
            act.dma_start(t["conv_sample"][0].rearrange("b w c -> (b w) c"), cst[0:24, :]).then_inc(s.out_misc, 16)
            act.dma_start(t["conv_prompt"][0, 0], cst[24:27, :]).then_inc(s.out_misc, 16)
            for grp in range(2):
                for m in range(32 * grp, 32 * grp + 32):
                    act.wait_ge(s.kt_ps, m + 1)
                    if m >= 2:
                        act.wait_ge(s.kpage_free, 4 + m - 1)
                    A_(kpT[:, m % 2], ps[:, 3 + m % 2, :].rearrange("p (c k) -> p c k", c=NPAIR),
                       ACT.Copy).then_inc(s.kt_done, 1)
                act.wait_ge(s.sa_max, grp + 1)
                A_(sS[:, 0:1056], ps[:, 0:3, :].rearrange("p a b -> p (a b)")[:, 0:1056], ACT.Exp, bias=pmax[:, 16 + grp:17 + grp],
                   accum_out=psm[:, 16 + grp:17 + grp]).then_inc(s.sa_exp, 1)
                act.wait_ge(s.sa_pt_ps, grp + 1)
                ch(A_(sPT[:, 0:8, :], ps[:, 5:7, :].rearrange("p a (b c) -> p (a b) c", c=P), ACT.Copy))
                A_(sPT[0:TS, 8, :], ps[0:TS, 7, 0:P], ACT.Copy).then_inc(s.sa_pt, 1)
            act.wait_ge(s.sa_o, 4)
            A_(dsq[:, :, :], cv[:, 0:8, :], ACT.Square).then_inc(s.dl_sq, 1)
            for j in range(8):
                act.wait_ge(s.dl_ss_ps, j + 1)
                A_(dsq[:, j, :], ps[:, j % 4, 0:T], ACT.Sqrt, scale=float(DB) if j < 4 else 1.0,
                   bias=epsq if j < 4 else epsb).then_inc(s.dl_rms, 1)
            for i in range(3):
                m = TOK[i][1]
                act.wait_ge(s.dl_R_ps, i + 1)
                src = ps[:, 3 + i, :].rearrange("p (h c) -> p h c", h=HB)[:, :, 0:m]
                A_(eR[:, i, :, 0:m], src, ACT.Exp).then_inc(s.dl_eR, 1)
            act.wait_ge(s.dl_cols, 1)
            ch(A_(egc, gcc, ACT.Exp))
            A_(kdc, kdc, ACT.Exp).then_inc(s.dl_cols, 1)
            for i in range(3):
                m = TOK[i][1]
                act.wait_ge(s.dl_dt, 4 * (i + 1))
                A_(dDT[0:m, i, :, 0:m], dDT[0:m, i, :, 0:m], ACT.Exp).then_inc(s.dl_dtx, 1)
            for h in range(HB):
                act.wait_ge(s.dl_o_ps, h + 1)
                A_(oT[:, h, :], ps[:, 6 + h % 2, 0:T], ACT.Copy).then_inc(s.dl_o, 1)
            act.wait_ge(s.dl_o, HB)
            A_(osq[:, :, :], oT[:, :, :], ACT.Square).then_inc(s.dl_osq, 1)
            for h in range(HB):
                act.wait_ge(s.dl_oss_ps, h + 1)
                A_(osq[:, h, :], ps[:, 2 + h, 0:T], ACT.Sqrt, scale=1.0 / DB, bias=epsb).then_inc(s.dl_orms, 1)
            act.wait_ge(s.dl_st_out, 1)
            act.dma_start(t["delta_prompt"][0, 0].rearrange("h k v -> k h v"), Sp[:, 1]).then_inc(s.out_misc, 16)
            act.wait_ge(s.dl_su, 8)
            act.dma_start(t["delta_sample"][0].rearrange("b h k v -> k (b h) v"), S0[:, :, :]).then_inc(s.out_misc, 16)

            def moe(layer, n_):
                act.wait_ge(s.x_new, 2 * layer + 1)
                norm_stats(n_)
                act.wait_ge(s.rt_e4x, 2 * layer + 1)
                A_(e4, d4, ACT.Exp).then_inc(s.rt_exp2, 1)
                act.wait_ge(s.rt_e4x, 2 * layer + 2)
                A_(ex2, ex2, ACT.Exp).then_inc(s.rt_exp2, 1)
                def iteration(li):
                    it = li + layer * ITERS
                    act.wait_ge(s.gs_ps, it + 1)
                    for e in range(2):
                        A_(gs[:, 4 * e:4 * e + 4, :], ps[:, 6 + e, 0:4 * C].rearrange("p (e c) -> p e c", e=4),
                           ACT.Copy).then_inc(s.gs_done, 1)
                    act.wait_ge(s.pt_ps, it + 1)
                    A_(pmT[0:C, :], ps[0:C, 4, 0:T], ACT.Copy).then_inc(s.pt_done, 1)
                    for e in range(EG):
                        act.wait_ge(s.gu_ps, it * EG + e + 1)
                        if e >= 2:
                            act.wait_ge(s.act_done, it * EG + e - 1)
                        A_(sg[:, e % 2], ps[:, 2 + e % 2, 0:FT * C].rearrange("p (f c) -> p f c", f=FT),
                           ACT.Silu).then_inc(s.silu_done, 1)
                    act.wait_ge(s.dn_used, (it + 1) * EG)
                    for hf in range(2):
                        A_(ysb[0:C, 512 * hf:512 * (hf + 1)], ps[0:C, 4 + hf, :], ACT.Copy).then_inc(s.ysb_done, 1)

                with act.Fori(0, NG) as li:
                    iteration(li)
                with act.If(more(act, layer) > 0):
                    with act.Fori(NG, ITERS) as li:
                        iteration(li)
                with act.Else():
                    skip_rounds(act, layer, (s.gs_done, 2), (s.pt_done, 1), (s.silu_done, EG), (s.ysb_done, 2))
            moe(0, 1)
            act.wait_ge(s.x_new, 2)
            norm_stats(2)
            act.dma_start(wsn[:, :, :], t["gm_spatial_w"][0].rearrange("h t s -> t h s")).then_inc(s.ws_loaded, 16)
            act.dma_start(bsr[0:1, :, 0:P], t["gm_spatial_b"]).then_inc(s.ws_loaded, 16)
            act.dma_start(lnw, t["gm_ln_w"][0:1, :].partition_broadcast(P)).then_inc(s.ws_loaded, 16)
            act.dma_start(lnb, t["gm_ln_b"][0:1, :].partition_broadcast(P)).then_inc(s.ws_loaded, 16)
            for j in range(8):
                for i, (r0, m) in enumerate(TOK):
                    act.wait_ge(s.gm_v_ps, 3 * j + i + 1)
                    A_(vrow[0:m, i, 256 * j:256 * (j + 1)], ps[0:m, 3 * (j % 2) + i, 0:256], ACT.Gelu,
                       accum_out=lsum[0:m, 8 * i + j:8 * i + j + 1]).then_inc(s.gm_v, 1)
            for c in range(NU):
                if c >= 1 and c <= 3:
                    i, m = c - 1, TOK[c - 1][1]
                    act.wait_ge(s.gm_sum, i + 1)
                    if i:
                        act.wait_ge(s.gm_sq, i)
                    A_(sqj[0:m, :], vrow[0:m, i, :], ACT.Square, accum_out=lss[0:m, i:i + 1]).then_inc(s.gm_sq, 1)
                if c == 3:
                    act.wait_ge(s.gm_sq, 3)
                    A_(lrs, lss, ACT.Sqrt, scale=1.0 / DC, bias=epsb).then_inc(s.gm_rms, 1)
                act.wait_ge(s.gm_u_ps, c + 1)
                A_(uT[:, c, :], ps[:, c % 4, 0:T], ACT.Gelu).then_inc(s.gm_u, 1)
            act.wait_ge(s.gm_vn, 3)
            act.dma_start(t["chunk_v"][0].rearrange("b l c -> (b l) c"), vrow[0:TS, 2, :]).then_inc(s.out_misc, 16)
            moe(1, 3)
            act.wait_ge(s.x_new, 4)
            norm_stats(4)
            act.dma_start(work[:, 0:D], t["norm_final"].rearrange("(o d) -> o d", o=1).partition_broadcast(P))\
                .then_inc(s.nf_loaded, 16)

        @block.vector
        def _(dve):
            V = nc.vector
            n = [0]

            def ch(ins):
                n[0] += 1
                ins.then_inc(s.dve_chain, 1)
                dve.wait_ge(s.dve_chain, n[0])

            def norm(n_):
                dve.wait_ge(s.rms_done, n_ + 1)
                ch(V.reciprocal(rr[:, 3 * n_:3 * n_ + 3], rms[:, 3 * n_:3 * n_ + 3]))
                for i, (r0, m) in enumerate(TOK):
                    V.tensor_scalar(htok[0:m, i, :], x[0:m, i, :], rr[0:m, 3 * n_ + i:3 * n_ + i + 1], None,
                                    ALU.mult).then_inc(s.h_ready, 1)
                if n_ == 4:
                    return
                for k in range(KD):
                    dve.wait_ge(s.hT_ps, KD * n_ + k + 1)
                    V.tensor_scalar(hT[:, k, :], ps[:, k % 4, 0:T], nw[:, n_, k:k + 1], None,
                                    ALU.mult).then_inc(s.hT_done, 1)

            V.memset(sm[:, 0:46], 1.0).then_inc(s.kpage_free, 4)
            dve.wait_ge(s.kpage_free, 4)
            ch(V.memset(htok[:, 2, :], 0.0))
            ch(V.memset(epsb, EPS))
            ch(V.memset(epsq, EPS * DB))
            ch(V.memset(fz, 0.0))
            ch(V.memset(lss, 1.0))
            ch(V.memset(gcc[:, 2, :], 0.0))
            ch(V.memset(kdc[:, 2, :], 0.0))
            V.memset(sm[:, 58:62], 0.0).then_inc(s.fz_sig, 1)
            dve.wait_ge(s.small_loaded, 16 * 16)
            norm(0)
            dve.wait_ge(s.fz_ps, 1)
            for i, (r0, m) in enumerate(TOK):
                V.tensor_copy(fz3[0:m, i, :], ps[0:m, 4, 16 * i:16 * i + 16]).then_inc(s.fz_copied, 1)
            dve.wait_ge(s.fz_copied, 3)
            ch(V.tensor_tensor(fz3, fz3, bc(biasrow.rearrange("p (o c) -> p o c", o=1), [P, 3, 16]), ALU.add))
            ch(V.tensor_scalar(fb, fz, -1.0, None, ALU.mult))
            V.tensor_tensor(fa, fz, fb, ALU.max).then_inc(s.fz_abs, 1)
            for c in range(NCT):
                last = V.memset(xc[:, c, 0:3], 0.0)
            ch(last)
            dve.wait_ge(s.fz_ln, 1)
            fb3 = fb.rearrange("p (t c) -> p t c", t=3)
            ch(V.scalar_tensor_tensor(lf, fz3[:, :, 0:8], 0.0, fb3[:, :, 0:8], ALU.min, ALU.subtract))
            ch(V.tensor_scalar(nlf, lf, -1.0, None, ALU.mult))
            ch(V.scalar_tensor_tensor(gg, fz3[:, :, 8:12], 0.0, fb3[:, :, 8:12], ALU.max, ALU.add))
            ch(V.scalar_tensor_tensor(gg, gg, -1.0, bc(expa.rearrange("p (o c) -> p o c", o=1), [P, 3, 4]),
                                      ALU.mult, ALU.mult))
            ch(V.tensor_scalar(beta, fz1.rearrange("p (t c) -> p t c", t=3)[:, :, 0:4], 1.0, None, ALU.add))
            ch(V.reciprocal(beta, beta))
            V.tensor_copy(lfn[0:TS, :].rearrange("p (b h q) -> p b h q", b=4, h=HA),
                          bc(nlf[0:TS, 2, :].rearrange("p (b h q) -> p b h q", b=1, q=1), [TS, 4, HA, QS]))\
                .then_inc(s.neglogf, 1)
            dve.wait_ge(s.cw_ps, 1)
            V.tensor_copy(cwc, ps[:, 6, 0:48]).then_inc(s.cw_done, 1)
            dve.wait_ge(s.cs_ps, 1)
            for c in range(NCT):
                last = V.tensor_copy(xc[:, c, XS:XC].rearrange("p (b w) -> p b w", b=NB)[:, :, 0:3],
                                     ps[:, 5, 24 * c:24 * c + 24].rearrange("p (b w) -> p b w", b=NB))
            last.then_inc(s.cs_copied, 1)
            dve.wait_ge(s.cw_done, 1)
            dve.wait_ge(s.cs_copied, 1)
            W_ = XC - 3
            for c in range(NCT):
                dve.wait_ge(s.proj_done, c + 1)
                for w in range(CW):
                    sc = cwc[:, w * NCT + c:w * NCT + c + 1]
                    src = xc[:, c, w:w + W_]
                    if w == 0:
                        ch(V.tensor_scalar(craw[:, c, 0:W_], src, sc, None, ALU.mult))
                    elif w < CW - 1:
                        ch(V.scalar_tensor_tensor(craw[:, c, 0:W_], src, sc, craw[:, c, 0:W_], ALU.mult, ALU.add))
                    else:
                        V.scalar_tensor_tensor(craw[:, c, 0:W_], src, sc, craw[:, c, 0:W_], ALU.mult, ALU.add)\
                            .then_inc(s.conv_raw, 1)
            ch(V.memset(qz[:, :, :], 0.0))
            dve.wait_ge(s.proj_done, 20)
            for b in range(NB):
                for c in range(NPAIR):
                    for e in range(2):
                        o = 32 * (b % 4) + 8 * c + 4 * e
                        last = V.tensor_copy(qz[64 * e:64 * e + 64, NPAIR * b + c, o:o + QS],
                                             qkT[64 * e:64 * e + 64, c, TP + QS * b:TP + QS * (b + 1)])
            ch(last)
            dve.wait_ge(s.conv_done, NCT)
            V.memset(sm[:, 500:501], 0.0).then_inc(s.vpage_free, 4)
            for j in range(6):
                i, (r0, m) = j // 2, TOK[j // 2]
                dve.wait_ge(s.kv_ps, j + 1)
                V.tensor_copy((ktok if j % 2 == 0 else vtok)[0:m, i, :], ps[0:m, j % 3, :]).then_inc(s.kv_copied, 1)
            dve.wait_ge(s.neglogf, 1)
            for h in range(HA + 1):
                if h < HA:
                    dve.wait_ge(s.pa_s_ps, h + 1)
                    for qb, c0, nk in ((0, 0, P), (1, P, TP)):
                        j = 2 * h + qb
                        V.tensor_reduce(pmax[:, j:j + 1], ps[:, h % 2, c0:c0 + nk], AX.X, ALU.max, negate=True)\
                            .then_inc(s.pa_max, 1)
                    for qb, c0, nk in ((0, 0, P), (1, P, TP)):
                        j = 2 * h + qb
                        dve.wait_ge(s.pa_exp, j + 1)
                        ch(V.reciprocal(pinv[:, j:j + 1], psm[:, j:j + 1]))
                        V.tensor_scalar(pP[:, h % 2, c0:c0 + nk], pP[:, h % 2, c0:c0 + nk], pinv[:, j:j + 1], None,
                                        ALU.mult).then_inc(s.pa_p, 1)
                if h:
                    g, o = h - 1, 64 * ((h - 1) % 2)
                    dve.wait_ge(s.pa_o_ps, h)
                    V.tensor_copy(mixT[o:o + 64, g // 2, 0:TP], ps[o:o + 64, 4 + g % 2, 0:TP]).then_inc(s.pa_o, 1)
                    if h == 1:
                        dve.wait_ge(s.cst_ps, 1)
                        V.tensor_copy(cst[0:27, :], ps[0:27, 5:8, :].rearrange("p a b -> p (a b)")).then_inc(s.cst_done, 1)
            for g in range(2):
                last = V.tensor_copy(eg[0:TS, g, :].rearrange("p (b h q) -> p b h q", b=4, h=HA),
                                     bc(ident[0:TS, 16 * g:16 * g + 16].rearrange("p (b h q) -> p b h q", h=1, q=QS),
                                        [TS, 4, HA, QS]))
            last.then_inc(s.qz_ready, 1)
            for grp in range(2):
                dve.wait_ge(s.bias_pages, 16 * 64)
                if grp:
                    dve.wait_ge(s.sa_s_ps, 1)
                V.tensor_scalar(lfx[:, :, :].rearrange("p n (b q) -> p (n b) q", q=QS),
                                bc(lfp[:, grp].rearrange("p n (b q) -> p (n b) q", q=1), [P, NPAGE * 32, QS]),
                                -1.0, None, ALU.mult).then_inc(s.ks_done, 1)
                dve.wait_ge(s.sa_s_ps, grp + 1)
                V.tensor_reduce(pmax[:, 16 + grp:17 + grp], ps[:, 0:3, :].rearrange("p a b -> p (a b)")[:, 0:1056],
                                AX.X, ALU.max, negate=True).then_inc(s.sa_max, 1)
                dve.wait_ge(s.sa_exp, grp + 1)
                ch(V.reciprocal(pinv[:, 16 + grp:17 + grp], psm[:, 16 + grp:17 + grp]))
                V.tensor_scalar(sS, sS, pinv[:, 16 + grp:17 + grp], None, ALU.mult).then_inc(s.sa_p, 1)
                dve.wait_ge(s.sa_o_ps, grp + 1)
                ov = ps[:, 7, 128:256].rearrange("p (b c j) -> p b c j", b=4, c=NPAIR)
                for e in range(2):
                    dst = mixT[64 * e:64 * e + 64, 0:NPAIR, TP + 16 * grp:TP + 16 * grp + 16]\
                        .rearrange("p c (b q) -> p b c q", b=4)
                    V.tensor_copy(dst, ov[64 * e:64 * e + 64, :, :, 4 * e:4 * e + 4]).then_inc(s.sa_o, 1)
            for j in range(8):
                dve.wait_ge(s.dl_rms, j + 1)
                ch(V.reciprocal(dsq[:, j, :], dsq[:, j, :]))
                V.tensor_tensor(cv[:, j, :], cv[:, j, :], dsq[:, j, :], ALU.mult).then_inc(s.dl_qk, 1)
            dve.wait_ge(s.out_misc, 16 * 11)
            for j in range(6):
                i, (r0, m) = j // 2, TOK[j // 2]
                dve.wait_ge(s.dl_tok_ps, j + 1)
                V.tensor_copy((ktok if j % 2 == 0 else vtok)[0:m, i, :], ps[0:m, j % 3, :]).then_inc(s.dl_tok, 1)
            dve.wait_ge(s.dl_cols_ps, 1)
            for i in range(3):
                m = TOK[i][1]
                ch(V.tensor_copy(gcc[0:m, i, :], ps[0:m, 6, 4 * i:4 * i + 4]))
                last = V.tensor_tensor(kdc[0:m, i, :], ps[0:m, 6, 16 + 4 * i:20 + 4 * i], gcc[0:m, i, :], ALU.subtract)
            last.then_inc(s.dl_cols, 1)
            dve.wait_ge(s.dl_eR, 3)
            for i in range(3):
                m = TOK[i][1]
                for h in range(HB):
                    V.scalar_tensor_tensor(dDT[0:m, i, h, 0:m], ps[0:m, 3 + i, P * h:P * h + m], gcc[0:m, i, h:h + 1],
                                           negT[:, :] if i < 2 else negTS, ALU.subtract, ALU.add,
                                           ).then_inc(s.dl_dt, 1)
            for i in range(3):
                m = TOK[i][1]
                dve.wait_ge(s.dl_kk_ps, i + 1)
                dve.wait_ge(s.dl_dtx, i + 1)
                for w, dst in ((0, dLT), (1, dQK)):
                    src = ps[0:m, w, :].rearrange("p (h c) -> p h c", h=HB)[:, :, 0:m]
                    V.tensor_tensor(dst[0:m, i, :, 0:m], src, dDT[0:m, i, :, 0:m], ALU.mult).then_inc(s.dl_kk, 1)
            dve.wait_ge(s.dl_kk, 6)
            idb = bc(ident[:, :].rearrange("p (o c) -> p o c", o=1), [P, HB, P])
            for i in range(3):
                ch(V.tensor_copy(dT[:, i], idb))
                last = V.tensor_copy(dTT[:, i], idb)
            last.then_inc(s.dl_t, 1)
            dve.wait_ge(s.dl_t, 1)
            nu, nt = 0, 1
            for l in range(7):
                for i in ((0, 1, 2) if l < 2 else (0, 1)):
                    m = TOK[i][1]
                    nu += 1
                    V.tensor_tensor(dMT[0:m, i, :, 0:m], dLT[0:m, i, :, 0:m],
                                    bc(lvl[0:m, l, 0:m].rearrange("p (o c) -> p o c", o=1), [m, HB, m]),
                                    ALU.mult).then_inc(s.dl_mt, 1)
                    dve.wait_ge(s.dl_u_ps, nu)
                    pv = lambda b: ps[0:m, b, :].rearrange("p (h c) -> p h c", h=HB)[:, :, 0:m]
                    V.tensor_tensor(dU[0:m, i, :, 0:m], pv(0),
                                    bc(beta[0:m, i, :].rearrange("p (h o) -> p h o", o=1), [m, HB, m]),
                                    ALU.mult).then_inc(s.dl_u, 1)
                    dve.wait_ge(s.dl_t_ps, nu)
                    V.tensor_tensor(dT[0:m, i, :, 0:m], dT[0:m, i, :, 0:m], pv(2), ALU.subtract).then_inc(s.dl_t, 1)
                    last = V.tensor_tensor(dTT[0:m, i, :, 0:m], dTT[0:m, i, :, 0:m], pv(4), ALU.subtract)
                    last.then_inc(s.dl_t, 1)
                    nt += 2
            dve.wait_ge(s.dl_t, nt)
            dve.wait_ge(s.dl_cols, 2)
            ch(V.tensor_tensor(bex, beta, egc, ALU.mult))
            for i in range(3):
                m = TOK[i][1]
                cb = lambda a: bc(a[0:m, i, :].rearrange("p (h o) -> p h o", o=1), [m, HB, P])
                V.tensor_tensor(vb[0:m, i], vdt[0:m, i], cb(beta), ALU.mult)
                ch(V.tensor_tensor(kbe[0:m, i], kdt[0:m, i], cb(bex), ALU.mult))
                last = V.tensor_tensor(kdt[0:m, i], kdt[0:m, i], cb(kdc), ALU.mult)
            last.then_inc(s.dl_scaled, 2)
            dve.wait_ge(s.dl_eR, 3)
            for i, (r0, m) in enumerate(TOK):
                last = V.tensor_tensor(cv[:, 0:HB, r0:r0 + m], cv[:, 0:HB, r0:r0 + m], eR[:, i, :, 0:m], ALU.mult)
            last.then_inc(s.dl_qdec, 1)
            for i in range(3):
                m = TOK[i][1]
                dve.wait_ge(s.dl_w_ps, i + 1)
                V.tensor_copy(wv[0:m, i], ps[0:m, 0, :].rearrange("p (h c) -> p h c", h=HB)).then_inc(s.dl_w, 1)
                V.tensor_copy(wkT[:, i, :, 0:m], ps[:, 1, :].rearrange("p (h c) -> p h c", h=HB)[:, :, 0:m])\
                    .then_inc(s.dl_w, 1)
            hv = lambda b: ps[:, b, :].rearrange("p (h c) -> p h c", h=HB)
            dve.wait_ge(s.dl_s_ps, 1)
            V.tensor_copy(Sp[:, 0], hv(2)).then_inc(s.dl_s, 1)
            dve.wait_ge(s.dl_v1_ps, 1)
            V.tensor_tensor(wv[:, 1], wv[:, 1], hv(3), ALU.subtract).then_inc(s.dl_v1, 1)
            ch(V.tensor_tensor(Sp[:, 1], Sp[:, 0], bc(eR[:, 1, :, P - 1:P], [P, HB, P]), ALU.mult))
            dve.wait_ge(s.dl_s_ps, 2)
            V.tensor_tensor(Sp[:, 1], Sp[:, 1], hv(2), ALU.add).then_inc(s.dl_st_out, 1)
            dve.wait_ge(s.dl_vs_ps, 1)
            V.tensor_copy(vsT, ps[:, 4, 0:HB * TS]).then_inc(s.dl_vsT, 1)
            dve.wait_ge(s.dl_vt_ps, 1)
            V.tensor_tensor(wv[0:TS, 2], wv[0:TS, 2], ps[0:TS, 5, :].rearrange("p (h c) -> p h c", h=HB),
                            ALU.subtract).then_inc(s.dl_vs, 1)
            dve.wait_ge(s.dl_vs, 1)
            dve.wait_ge(s.dl_o_ps, HB)
            for b in range(NB):
                V.tensor_scalar(vexp[0:TS, b, :], wv[0:TS, 2].rearrange("p h e -> p (h e)"), bsel[:, b:b + 1], None,
                                ALU.mult).then_inc(s.dl_vexp, 1)
            S04 = S0.rearrange("p (b h) e -> p b h e", h=HB)
            for h in range(HB):
                last = V.tensor_tensor(S04[:, :, h, :], S04[:, :, h, :],
                                       bc(eR[:, 2, h, QS - 1:TS:QS].rearrange("p (b o) -> p b o", o=1), [P, NB, P]),
                                       ALU.mult)
            ch(last)
            for j in range(8):
                h, q = j // 2, j % 2
                dve.wait_ge(s.dl_su_ps, j + 1)
                V.tensor_tensor(S04[:, 4 * q:4 * q + 4, h, :], S04[:, 4 * q:4 * q + 4, h, :],
                                ps[:, j % 2, :].rearrange("p (b e) -> p b e", b=4), ALU.add).then_inc(s.dl_su, 1)
            dve.wait_ge(s.dl_orms, HB)
            ch(V.reciprocal(osq, osq))
            ch(V.tensor_tensor(oT, oT, osq, ALU.mult))
            for h in range(HB):
                V.scalar_tensor_tensor(mixT[:, 4 + h, :], oT[:, h, :], onw, gT[:, h, :], ALU.mult,
                                       ALU.mult).then_inc(s.dl_mixed, 1)

            def add_out(used, sem_value):
                dve.wait_ge(s.w_used, used)
                for i, (r0, m) in enumerate(TOK):
                    for hf in range(2):
                        last = V.tensor_tensor(x[0:m, i, 512 * hf:512 * (hf + 1)], x[0:m, i, 512 * hf:512 * (hf + 1)],
                                               ps[0:m, 2 * i + hf, :], ALU.add)
                last.then_inc(s.x_new, 1)
                dve.wait_ge(s.x_new, sem_value)

            add_out(4, 1)

            def first_of(dst, eq, width, base):
                rv = bc(rev[:, NE - width:NE].rearrange("p (o c) -> p o c", o=1), [P, 3, width])
                ch(V.tensor_tensor(eq, eq, rv, ALU.mult))
                ch(V.tensor_reduce(mr, eq, AX.X, ALU.max))
                ch(V.tensor_tensor(dst, eq, bc(mr, [P, 3, width]), ALU.is_equal))

            def moe(layer, n_):
                norm(n_)
                dve.wait_ge(s.rl_ps, layer + 1)
                dve.wait_ge(s.out_misc, 16 * 13)
                ch(V.memset(lg, 0.0))
                for i, (r0, m) in enumerate(TOK):
                    ch(V.tensor_copy(lg[0:m, i, :], ps[0:m, 4, 36 * i:36 * i + 36]))
                ch(V.tensor_reduce(m4, lg[:, :, 0:NG], AX.X, ALU.max))
                V.tensor_tensor(d4, lg[:, :, 0:NG], bc(m4, [P, 3, NG]), ALU.subtract).then_inc(s.rt_e4x, 1)
                dve.wait_ge(s.rt_e4x, 2 * layer + 1)
                ch(V.tensor_scalar(eq4, d4, 0.0, None, ALU.is_ge))
                dve.wait_ge(s.rt_exp2, 2 * layer + 1)
                ch(V.tensor_reduce(s4, e4, AX.X, ALU.add))
                first_of(oh4, eq4, NG, 0)
                ch(V.tensor_scalar(pen, oh4, BIG, -BIG, ALU.mult, ALU.add))
                for g in range(NG):
                    last = V.tensor_tensor(lem[:, :, EG * g:EG * (g + 1)], lg[:, :, NG + EG * g:NG + EG * (g + 1)],
                                           bc(pen[:, :, g:g + 1], [P, 3, EG]), ALU.add)
                last.then_inc(s.rt_oh, 1)
                dve.wait_ge(s.rt_oh, layer + 1)
                ch(V.tensor_reduce(v1, lem, AX.X, ALU.max))
                ch(V.tensor_tensor(eqa, lem, bc(v1, [P, 3, NE]), ALU.is_equal))
                first_of(oh1, eqa, NE, 0)
                ch(V.scalar_tensor_tensor(lem, oh1, -2.0 * BIG, lem, ALU.mult, ALU.add))
                ch(V.tensor_reduce(v2, lem, AX.X, ALU.max))
                ch(V.tensor_tensor(eqa, lem, bc(v2, [P, 3, NE]), ALU.is_equal))
                first_of(oh2, eqa, NE, 0)
                V.tensor_tensor(ex2, v2, v1, ALU.subtract).then_inc(s.rt_e4x, 1)
                dve.wait_ge(s.rt_exp2, 2 * layer + 2)
                ch(V.tensor_scalar(w1, ex2, 1.0, None, ALU.add))
                ch(V.tensor_tensor(w1, w1, s4, ALU.mult))
                ch(V.reciprocal(w1, w1))
                ch(V.tensor_tensor(w2, w1, ex2, ALU.mult))
                ch(V.tensor_tensor(oh1, oh1, bc(w1, [P, 3, NE]), ALU.mult))
                ch(V.tensor_tensor(oh2, oh2, bc(w2, [P, 3, NE]), ALU.mult))
                ch(V.tensor_tensor(oh1, oh1, oh2, ALU.add))
                ch(V.tensor_tensor(oh2[:, :, 0:16], oh1[:, :, 0:16], oh1[:, :, 16:32], ALU.add))
                ch(V.tensor_tensor(g8, oh2[:, :, 0:8], oh2[:, :, 8:16], ALU.add))
                dve.wait_ge(s.rank_ps, layer + 1)
                ch(V.tensor_reduce(gmax, ps[0:1, 5, 16:20], AX.X, ALU.max))
                V.tensor_scalar(flag[:, layer:layer + 1], gmax, float(C), None, ALU.is_gt).then_inc(s.flag_ready, 1)
                ch(V.memset(rk, 0.0))
                for i, (r0, m) in enumerate(TOK):
                    ch(V.tensor_copy(rk[0:m, i, :], ps[0:m, 5, 4 * i:4 * i + 4]))
                ch(V.tensor_scalar(rk2, rk, float(C), float((NG - 1) * C), ALU.is_gt, ALU.mult))
                ch(V.tensor_scalar(eq4, rk, float(2 * C), float((NG - 1) * C), ALU.is_gt, ALU.mult))
                ch(V.tensor_tensor(rk, rk, rk2, ALU.add))
                ch(V.tensor_tensor(rk, rk, eq4, ALU.add))
                for g in range(NG):
                    last = V.tensor_scalar(rk[:, :, g:g + 1], rk[:, :, g:g + 1], float(C * g - 1), None, ALU.add)
                ch(last)
                ch(V.tensor_tensor(rk, rk, oh4, ALU.mult))
                ch(V.tensor_reduce(pos, rk, AX.X, ALU.add))
                ch(V.memset(pm[:, 2, :], 0.0))
                V.tensor_copy(iota[:, 1, :], iota[:, 0, :]).then_inc(s.rank_done, 1)
                dve.wait_ge(s.rank_done, layer + 1)
                def iteration(li):
                    it = li + layer * ITERS
                    for i, (r0, m) in enumerate(TOK):
                        V.tensor_scalar(pm[0:m, i, :], iota[0:m, 1, :], pos[0:m, i, :], None,
                                        ALU.is_equal).then_inc(s.perm_ready, 1)
                    dve.wait_ge(s.hg_ps, it + 1)
                    for k in range(2):
                        V.tensor_tensor(hg[:, 4 * k:4 * k + 4, :], ps[:, k, 0:4 * C].rearrange("p (k c) -> p k c", k=4),
                                        bc(nw[:, n_, 4 * k:4 * k + 4].rearrange("p (k o) -> p k o", o=1), [P, 4, C]),
                                        ALU.mult).then_inc(s.hg_done, 1)
                    dve.wait_ge(s.gs_done, 2 * it + 2)
                    for e in range(EG):
                        dve.wait_ge(s.silu_done, it * EG + e + 1)
                        V.tensor_tensor(a1[:, e % 2], ps[:, 2 + e % 2, FT * C:2 * FT * C]
                                        .rearrange("p (f c) -> p f c", f=FT), sg[:, e % 2], ALU.mult)\
                            .then_inc(s.moe_chain, 1)
                        dve.wait_ge(s.moe_chain, it * (EG + 1) + e + 1)
                        if e >= 2:
                            dve.wait_ge(s.dn_used, it * EG + e - 1)
                        V.tensor_tensor(av[:, e % 2], a1[:, e % 2],
                                        bc(gs[:, e, :].rearrange("p (o c) -> p o c", o=1), [P, FT, C]),
                                        ALU.mult).then_inc(s.act_done, 1)
                    V.tensor_scalar(iota[:, 1, :], iota[:, 1, :], float(C), None, ALU.add).then_inc(s.moe_chain, 1)
                    for j in range(6):
                        i, (r0, m) = j // 2, TOK[j // 2]
                        xs = x[0:m, i, 512 * (j % 2):512 * (j % 2 + 1)]
                        dve.wait_ge(s.sc_ps, it * 6 + j + 1)
                        V.tensor_tensor(xs, xs, ps[0:m, (0, 1, 6, 7)[j % 4], :], ALU.add).then_inc(s.xadd, 1)
                    dve.wait_ge(s.moe_chain, it * (EG + 1) + EG + 1)
                    dve.wait_ge(s.xadd, it * 6 + 6)

                with dve.Fori(0, NG) as li:
                    iteration(li)
                with dve.If(more(dve, layer) > 0):
                    with dve.Fori(NG, ITERS) as li:
                        iteration(li)
                with dve.Else():
                    skip_rounds(dve, layer, (s.perm_ready, 3), (s.hg_done, 2), (s.moe_chain, EG + 1), (s.act_done, EG), (s.xadd, 6))
                V.memset(cwc[:, 0:1], 0.0).then_inc(s.x_new, 1)

            moe(0, 1)
            norm(2)
            for h in range(HC):
                dve.wait_ge(s.ws_ps, 4 * (h // 4 + 1))
                V.tensor_tensor(wmT[:, h, :], ps[:, 6, P * (h % 4):P * (h % 4 + 1)], ut, ALU.mult).then_inc(s.ws_done, 1)
            V.tensor_copy(rep[0:QS], bc(ident[0:QS, 0:QS].rearrange("p (o q) -> p o q", o=1), [QS, NB, QS]))\
                .then_inc(s.ws_done, 1)
            dve.wait_ge(s.ws_loaded, 64)
            ch(V.tensor_copy(bsr[0:1, :, P:TP], bsr[0:1, :, 0:P]))
            for b in range(NB):
                last = V.tensor_copy(bsr[0:1, :, TP + QS * b:TP + QS * (b + 1)], bsr[0:1, :, 0:QS])
            last.then_inc(s.gm_bias, 1)
            dve.wait_ge(s.wrep_ps, 1)
            ch(V.tensor_copy(wrep[0:TS, :], ps[0:TS, 7, 0:HC * QS]))
            for h in range(HC):
                V.tensor_tensor(wS[0:TS, h, :].rearrange("p (b q) -> p b q", b=NB),
                                bc(wrep[0:TS, QS * h:QS * (h + 1)].rearrange("p (o q) -> p o q", o=1), [TS, NB, QS]),
                                same.rearrange("p (b q) -> p b q", b=NB), ALU.mult).then_inc(s.wrep_done, 1)
            dve.wait_ge(s.gm_v, 24)
            for i, (r0, m) in enumerate(TOK):
                ch(V.tensor_reduce(lmu[0:m, i:i + 1], lsum[0:m, 8 * i:8 * i + 8], AX.X, ALU.add))
                ch(V.tensor_scalar(lmu[0:m, i:i + 1], lmu[0:m, i:i + 1], 1.0 / DC, None, ALU.mult))
                V.tensor_scalar(vrow[0:m, i, :], vrow[0:m, i, :], lmu[0:m, i:i + 1], None,
                                ALU.subtract).then_inc(s.gm_sum, 1)
            dve.wait_ge(s.gm_rms, 1)
            ch(V.reciprocal(lrs, lrs))
            for i, (r0, m) in enumerate(TOK):
                ch(V.scalar_tensor_tensor(vrow[0:m, i, :], vrow[0:m, i, :], lrs[0:m, i:i + 1], lnw[0:m, :],
                                          ALU.mult, ALU.mult))
                V.tensor_tensor(vrow[0:m, i, :], vrow[0:m, i, :], lnb[0:m, :], ALU.add).then_inc(s.gm_vn, 1)
            dve.wait_ge(s.gm_u, NU)
            for c in range(NU):
                dve.wait_ge(s.gm_m_ps, c + 1)
                V.tensor_tensor(uT[:, c, :], uT[:, c, :], ps[:, c % 4, 0:T], ALU.mult).then_inc(s.gm_m, 1)
            add_out(12, 3)
            moe(1, 3)
            norm(4)
            dve.wait_ge(s.nf_loaded, 16)
            dve.wait_ge(s.h_ready, 15)
            for i, (r0, m) in enumerate(TOK):
                V.tensor_tensor(htok[0:m, i, :], htok[0:m, i, :], work[0:m, 0:D], ALU.mult).then_inc(s.fin_y, 1)


OUTS = [("y_prompt", (1, TP, D)), ("y_sample", (NB, QS, D)), ("k_prompt", (1, 1, TP, HA, DA)),
        ("v_prompt", (1, 1, TP, HA, DA)), ("logf_prompt", (1, 1, TP, HA)), ("delta_prompt", (1, 1, HB, DB, DB)),
        ("conv_prompt", (1, 1, CW - 1, NCT * P)), ("k_sample", (1, NB, QS, HA, DA)), ("v_sample", (1, NB, QS, HA, DA)),
        ("logf_sample", (1, NB, QS, HA)), ("delta_sample", (1, NB, HB, DB, DB)),
        ("conv_sample", (1, NB, CW - 1, NCT * P)), ("chunk_v", (1, NB, QS, DC))]


def kernel(**inputs):
    import numpy as np
    import concourse.bacc as bacc
    from concourse.bass_utils import run_bass_kernel_spmd

    nc = bacc.Bacc("TRN2", target_bir_lowering=False, num_devices=1, dynamic_dma_scratch_size=2048)
    arrays, t = {}, {}
    for name, value in inputs.items():
        a = np.ascontiguousarray(value)
        arrays[f"in_{name}"] = a
        t[name] = nc.dram_tensor(f"in_{name}", a.shape, mybir.dt.from_np(a.dtype), kind="ExternalInput").ap()
    for name, shape in OUTS:
        t[name] = nc.dram_tensor(f"out_{name}", shape, F32, kind="ExternalOutput").ap()
    build(nc, t)
    r = run_bass_kernel_spmd(nc, [arrays], core_ids=[0])
    return tuple(r.results[0][f"out_{name}"] for name, _ in OUTS)
```

```python
from contextlib import ExitStack

import concourse.bass as bass
from concourse import mybir

F32 = mybir.dt.float32
I32 = mybir.dt.int32
ALU = mybir.AluOpType
ACT = mybir.ActivationFunctionType
AX = mybir.AxisListType

P = 128
D = 1024
KD = D // P
TP, NB, QS = 256, 8, 4
TS = NB * QS
T = TP + TS
TOK = [(0, 128), (128, 128), (256, TS)]
EPS = 1e-6
HA, DA = 8, 64
NPAIR = HA // 2
NPAGE, PG = 8, 128
HB, DB = 4, 128
CW = 4
NCT = 12
XC = (CW - 1) + TP + NB * (CW - 1 + QS)
XS = CW - 1 + TP
BIG = 1.0e30
NG, EG = 4, 8
NE = NG * EG
DE = 256
FT = DE // P
C = 96
ROUNDS = T // C
ITERS = ROUNDS * NG
XADD0 = 2
SMALL, REST = 9, 7
GCOL = 3 * P
SLOTS = 8
UNIT = 2048
EVEN_UNITS, ODD_UNITS, MOE_UNITS = 18, 24, 3 * EG
DC = 2048
NU = DC // P
HC = 8

SEMS = """x_loaded small_loaded rest_loaded pagetab_loaded consts ss_done rms_done h_ready hT_ps hT_done fz_ps fz_copied
 fz_abs fz_ln fz_sig proj_ps proj_done w_used kv_ps kv_copied cs_ps cs_copied cs27 cst_ps cst_done cw_ps cw_done
 conv_raw conv_done neglogf qz_ready pa_s_ps pa_max pa_exp pa_p pa_pt_ps pa_pt pa_o_ps pa_o kpage_free
 vpage_free kt_ps kt_done ks_done bias_pages sa_s_ps sa_max sa_exp sa_p sa_pt_ps sa_pt sa_o_ps sa_o s0_loaded
 dl_sq dl_ss_ps dl_rms dl_qk dl_tok_ps dl_tok dl_R_ps dl_eR dl_cols_ps dl_cols dl_dt dl_dtx dl_kk_ps dl_kk dl_mt
 dl_u_ps dl_u dl_t_ps dl_t dl_scaled dl_w_ps dl_w dl_qdec dl_v1_ps dl_v1 dl_s_ps dl_s dl_vs_ps dl_vsT dl_vt_ps
 dl_vs dl_o_ps dl_o dl_osq dl_oss_ps dl_orms dl_mixed dl_vexp dl_su_ps dl_su dl_st_out x_new ws_loaded ws_ps
 ws_done wrep_ps wrep_done gm_v_ps gm_v gm_u_ps gm_u gm_sum gm_sq gm_rms gm_vn gm_bias gm_m_ps gm_m rl_ps rt_e4x
 rt_exp2 rt_oh rank_ps rank_done flag_ready perm_ready hg_ps hg_done gs_ps gs_done pt_ps pt_done g_used gu_ps
 silu_done act_done dn_used ysb_done sc_ps xadd fin_y nf_loaded out_misc dve_chain act_chain pool_chain
 moe_chain""".split()


class Named(dict):
    __getattr__ = dict.__getitem__


def build(nc, t):
    ctx = ExitStack()
    with ctx:
        def sb(name, shape, dt=F32):
            return ctx.enter_context(nc.sbuf_tensor(name, shape, dt))

        s = Named({n: ctx.enter_context(nc.semaphore(n)) for n in SEMS})
        s_w = [ctx.enter_context(nc.semaphore(f"w_slot{i}")) for i in range(SLOTS)]
        s_k = [ctx.enter_context(nc.semaphore(f"k_slot{i}")) for i in range(4)]
        s_v = [ctx.enter_context(nc.semaphore(f"v_slot{i}")) for i in range(4)]

        ps = ctx.enter_context(nc.psum_tensor("ps", [P, 8, 512], F32))

        x = sb("x", [P, 3, D])
        htok = sb("htok", [P, 3, D])
        hT = sb("hT", [P, KD, T])
        ring = sb("ring", [P, SLOTS, UNIT])
        vring = ring[:, 2:6, :].rearrange("p s (n c) -> p (s n) c", n=4)
        work = sb("work", [P, 23700])
        cum = sb("cum", [P, 1408])
        ident = sb("ident", [P, P])
        negq = sb("negq", [P, P])
        negT = sb("negT", [P, P])
        lvl = sb("lvl", [P, 7, P])
        msk = sb("msk", [TS, 5, TS])
        iota = sb("iota", [P, 2, C])
        rev = sb("rev", [P, NE])
        nw = sb("nw", [P, 5, KD])
        sm = sb("sm", [P, 520])
        wsm = sb("wsm", [P, KD, 16])
        wr = sb("wr", [P, 2, KD, NG + NE])
        ptab = sb("ptab", [1, NB * NPAGE], I32)
        flag = sb("flag", [1, 2], I32)
        lfp = sb("lfp", [P, 2, NPAGE, 32])
        cs27 = sb("cs27", [P, NCT, 27])
        cst = sb("cst", [27, NCT * P])
        lfn = sb("lfn", [TS, P])

        ut, one = cum[:, 384:512], cum[:, 512:640]
        same, utS, negTS, negQS = (msk[:, i, :] for i in range(4))
        bsel = msk[:, 4, 0:NB]

        def col(i, n=1):
            return sm[:, i:i + n]

        ss, rms, rr, epsb = col(0, 15), col(15, 15), col(30, 15), col(45)
        biasrow, alog, expa, fz = col(46, 16), col(62, 4), col(66, 4), col(70, 48)
        fz3 = fz.rearrange("p (t c) -> p t c", t=3)
        fa = col(118, 48)
        fb = col(166, 48)
        lf = col(214, 24).rearrange("p (t h) -> p t h", t=3)
        nlf = col(238, 24).rearrange("p (t h) -> p t h", t=3)
        gg = col(262, 12).rearrange("p (t h) -> p t h", t=3)
        beta = col(274, 12).rearrange("p (t h) -> p t h", t=3)
        gcc = col(286, 12).rearrange("p (t h) -> p t h", t=3)
        egc = col(298, 12).rearrange("p (t h) -> p t h", t=3)
        kdc = col(310, 12).rearrange("p (t h) -> p t h", t=3)
        bex = col(322, 12).rearrange("p (t h) -> p t h", t=3)
        onw = col(334)
        pmax, psm, pinv = col(335, 20), col(355, 20), col(375, 20)
        cwc = col(395, 48)
        lsum = col(118, 48)
        lmu, lss, lrs = col(467, 3), col(470, 3), col(473, 3)
        epsq = col(476)
        fz1 = col(477, 24)

        def wk(off, *dims):
            n = 1
            for d in dims:
                n *= d
            a = work[:, off:off + n]
            if len(dims) == 2:
                return a.rearrange("p (a b) -> p a b", a=dims[0])
            if len(dims) == 3:
                return a.rearrange("p (a b c) -> p a b c", a=dims[0], b=dims[1])
            return a

        qkT = wk(0, 8, T)
        xc = wk(2304, NCT, XC)
        cv = wk(6084, NCT, T)
        gT = wk(9540, HB, T)
        A = 10692
        qz = wk(A, NB * NPAIR, P)
        kring = wk(A + 4096, 4, 512)
        kpT = wk(A + 6144, 2, NPAIR, P)
        dsq = wk(A + 7168, 8, T)
        sS = wk(A + 9472, 1056)
        sO = sS[:, 0:512]
        sPT = wk(A + 10528, 9, P)
        lfx, acx = wk(A + 9472, NPAGE, P), wk(A + 10528, NPAGE, P)
        acc = wk(A + 11680, 2, NPAGE * 32)
        pP = wk(A + 11424, 2, 384)
        pPT = wk(A + 12192, 2, 384)
        vT = wk(A + 11424, 4, T)
        craw = wk(A + 7168, NCT, XC)
        scin = wk(A + 10948, NCT * P)
        cwr = wk(A + 12484, P)
        ktok = htok[:, :, 0:512]
        vtok = htok[:, :, 512:1024]
        mixT = hT
        S0 = wk(0, NB * HB, P)
        dU = wk(A, 3, HB, P)
        dDT = dU
        dMT = wk(A + 1536, 3, HB, P)
        dT = wk(A + 3072, 3, HB, P)
        vexp = wk(A, NB, HB * P)
        dLT = wk(A + 4608, 3, HB, P)
        dQK = wk(A + 6144, 3, HB, P)
        dTT = wk(A + 7680, 3, HB, P)
        eR = wk(A + 9216, 3, HB, P)
        oT = wk(A + 10752, HB, T)
        Sp = wk(A + 11904, 2, HB, P)
        kdt = htok[:, :, 0:512].rearrange("p t (h e) -> p t h e", h=HB)
        vdt = htok[:, :, 512:1024].rearrange("p t (h e) -> p t h e", h=HB)
        kbe, vb, wkT, wv = dU, dMT, dT, dLT
        osq = wk(A + 6144, HB, T)
        vsT = wk(A + 1536, HB * TS)
        eg = wk(A + 12704, 2, P)
        vrow = wk(0, 3, DC)
        uT = wk(6144, NU, T)
        lnw = wk(10752, DC)
        lnb = wk(12800, DC)
        nfw = wk(10752, D)
        wmT = wk(14848, HC, P)
        wsn = wk(15872, HC, P)
        vg = wk(16896, 4, T)
        sqj = wk(18496, DC)
        bsr = wk(18496 + DC, HC, T)
        wrep = wk(15872, HC * QS)
        wS = wk(15904, HC, TS)
        rep = wk(16160, NB, QS)
        M = 18496
        hg = wk(M, KD, C)
        pm = wk(M + 768, 3, C)
        pmT = wk(M + 1056, T)
        gs = wk(M + 1344, EG, C)
        sg = wk(M + 2112, 2, FT, C)
        a1 = wk(M + 2496, 2, FT, C)
        av = wk(M + 2880, 2, FT, C)
        ysb = wk(M + 3264, D)
        dg = wk(M + 3264, EG, C)
        gsr = col(512, EG)
        rt = wk(M + 4288, 3, 212)
        lg = rt[:, :, 0:36]
        d4, e4, eq4, oh4, pos = rt[:, :, 36:40], rt[:, :, 40:44], rt[:, :, 44:48], rt[:, :, 48:52], rt[:, :, 52:53]
        m4, s4, mr, v1, v2, w1, w2, ex2 = (rt[:, :, 53 + i:54 + i] for i in range(8))
        gmax = rt[0:1, 0, 75:76]
        rk, rk2 = rt[:, :, 62:66], rt[:, :, 66:70]
        pen = rt[:, :, 70:74]
        lem, eqa, oh1, oh2 = (rt[:, :, 76 + 32 * i:108 + 32 * i] for i in range(4))
        g8 = rt[:, :, 204:212]

        def bc(ap, shape):
            return ap.to_broadcast(shape)

        zero512 = bc(cum[:, 0:1], [P, 512])

        w_in = t["w_in_even"][0].rearrange("(p k) c -> p k c", k=KD)
        w_oe = t["w_out_even"][0].rearrange("(c p) d -> p c d", p=P)
        w_io = t["w_in_odd"][0].rearrange("(p k) c -> p k c", k=KD)
        w_oo = t["w_out_odd"][0].rearrange("(c p) d -> p c d", p=P)
        WG, WU, WD = t["moe_w_gate"], t["moe_w_up"], t["moe_w_down"]
        COLS = [1544 + c * 256 for c in range(6)] + [3088, 3344] + [c * 256 for c in range(6)]
        even_src = [w_in[:, :, c:c + 256] for c in COLS] + [w_oe[:, 2 * i:2 * i + 2, :] for i in range(4)]
        odd_src = [w_io[:, :, DC + 256 * i:DC + 256 * (i + 1)] for i in range(8)] \
            + [w_io[:, :, 256 * i:256 * (i + 1)] for i in range(8)] + [w_oo[:, 2 * i:2 * i + 2, :] for i in range(8)]

        def kview(u):
            return ring[:, u % SLOTS, :].rearrange("p (k c) -> p k c", k=KD)

        def cview(u):
            return ring[:, u % SLOTS, :].rearrange("p (c d) -> p c d", c=2)

        MOE0 = [EVEN_UNITS, EVEN_UNITS + ITERS * MOE_UNITS + ODD_UNITS]
        ODD0 = EVEN_UNITS + ITERS * MOE_UNITS

        def wait_unit(eng, u, it=0):
            eng.wait_ge(s_w[u % SLOTS], 16 * (u // SLOTS + 1) + it * (16 * MOE_UNITS // SLOTS))

        def more(eng, layer):
            eng.wait_ge(s.flag_ready, layer + 1)
            return eng.value_load(flag[0:1, layer:layer + 1], min_val=0, max_val=1)

        def skip_rounds(eng, layer, *counts):
            for sm_, per in counts:
                eng.wait_ge(sm_, (layer * ITERS + NG) * per)
                eng.sem_inc(sm_, (ITERS - NG) * per)

        def v_chan(c):
            return c + 1 + max(c - 2, 0)

        def v_rows(c):
            return min(c + 3, NU) + c + 1

        def inv_tiles(l):
            return (0, 1, 2) if l < 2 else (0, 1)

        def inv_no(l, i):
            return 3 * min(l, 2) + 2 * max(l - 2, 0) + i + 1

        def inv_ps(i, w):
            m = TOK[i][1]
            if i < 2:
                return ps[:, 2 * w + i, :].rearrange("p (h c) -> p h c", h=HB)
            return ps[0:m, 6 + (w > 0), (w == 2) * P:(w == 2) * P + HB * m].rearrange("p (h c) -> p h c", h=HB)

        block = ctx.enter_context(nc.Block())

        @block.sync
        def _(sp):
            for i, (r0, n) in enumerate(TOK):
                src = t["x_prompt"][0, r0:r0 + n, :] if i < 2 else t["x_sample"].rearrange("b q d -> (b q) d")
                sp.dma_start(x[0:n, i, :], src).then_inc(s.x_loaded, 16)

            def load(u, src, it=0):
                sp.dma_start(ring[:, u % SLOTS, :].rearrange("p (a b) -> p a b", a=src.shape[1]) if len(src.shape) == 3
                             else ring[:, u % SLOTS, :], src).then_inc(s_w[u % SLOTS], 16)

            def even_used(u):
                if u < 14:
                    sp.wait_ge(s.proj_ps, 2 * (u + 1))
                else:
                    sp.wait_ge(s.w_used, u - 13)

            def odd_used(j):
                if j < 8:
                    sp.wait_ge(s.gm_v_ps, v_chan(2 * j + 1))
                elif j < 16:
                    sp.wait_ge(s.gm_u_ps, 2 * (j - 7))
                else:
                    sp.wait_ge(s.w_used, 4 + j - 15) if j < 23 else sp.wait_ge(s.gm_m_ps, NU + 8)

            def moe_used(layer, it, j):
                n = (it + layer * ITERS) * EG + j // 3 + 1
                sp.wait_ge((s.g_used, s.gu_ps, s.dn_used)[j % 3], n)

            def moe_load(layer, group, it, j):
                e = group * EG + j // 3
                w = (WG, WU, WD)[j % 3][layer, bass.ds(e, 1)]
                load(MOE0[layer] + j, w.rearrange("e (p k) f -> p (e k f)", p=P))

            for u in range(EVEN_UNITS):
                if u >= SLOTS:
                    even_used(u - SLOTS)
                load(u, even_src[u])
            sp.wait_ge(s.pagetab_loaded, 16)
            ck = t["cache_k"][0]
            with sp.Fori(0, NB) as b:
                for pg in range(NPAGE):
                    page = sp.value_load(ptab[0:1, bass.ds(b * NPAGE + pg, 1)], min_val=0, max_val=ck.shape[0] - 1)
                    sp.wait_ge(s.kpage_free, b * NPAGE + (pg + 1))
                    sp.dma_start(kring[:, pg % 4, :], ck[bass.ds(page, 1)]
                                 .rearrange("a r h d -> r (a h d)")).then_inc(s_k[pg % 4], 16)
            sp.wait_ge(s.sa_o, 6)
            sp.wait_ge(s.pa_o, HA)
            sp.dma_start(S0[:, :, :], t["state_delta"][0].rearrange("b h k v -> k (b h) v")).then_inc(s.s0_loaded, 16)
            for layer in range(2):
                for j in range(SLOTS):
                    if layer == 0:
                        even_used(EVEN_UNITS - SLOTS + j)
                    else:
                        odd_used(ODD_UNITS - SLOTS + j)
                    moe_load(layer, 0, 0, j)

                def first_groups(r):
                    with sp.Fori(0, NG - 1) as g:
                        it = g + r * NG
                        for j in range(SLOTS, MOE_UNITS + SLOTS):
                            moe_used(layer, it, j - SLOTS)
                            if j < MOE_UNITS:
                                moe_load(layer, g, it, j)
                            else:
                                moe_load(layer, g + 1, it + 1, j - MOE_UNITS)

                def last_group(r, last):
                    it = r * NG + NG - 1
                    for j in range(SLOTS, MOE_UNITS + (0 if last else SLOTS)):
                        moe_used(layer, it, j - SLOTS)
                        if j < MOE_UNITS:
                            moe_load(layer, NG - 1, it, j)
                        else:
                            moe_load(layer, 0, it + 1, j - MOE_UNITS)

                first_groups(0)
                with sp.If(more(sp, layer) > 0):
                    last_group(0, False)
                    for r in range(1, ROUNDS):
                        first_groups(r)
                        last_group(r, r == ROUNDS - 1)
                with sp.Else():
                    last_group(0, True)
                    for k in range(SLOTS):
                        u = MOE0[layer] + NG * MOE_UNITS - SLOTS + k
                        wait_unit(sp, u)
                        sp.sem_inc(s_w[u % SLOTS], 16 * (ITERS - NG) * MOE_UNITS // SLOTS)
                if layer == 0:
                    for j in range(ODD_UNITS):
                        if j < SLOTS:
                            moe_used(0, ITERS - 1, MOE_UNITS - SLOTS + j)
                        else:
                            odd_used(j - SLOTS)
                        load(ODD0 + j, odd_src[j])
            sp.wait_ge(s.fin_y, 1)
            sp.dma_start(t["y_prompt"][0, 0:P, :], htok[:, 0, :]).then_inc(s.out_misc, 16)
            sp.wait_ge(s.fin_y, 2)
            sp.dma_start(t["y_prompt"][0, P:TP, :], htok[:, 1, :]).then_inc(s.out_misc, 16)
            sp.wait_ge(s.fin_y, 3)
            sp.dma_start(t["y_sample"].rearrange("b q d -> (b q) d"), htok[0:TS, 2, :]).then_inc(s.out_misc, 16)
            sp.wait_ge(s.out_misc, 16 * 17)

        @block.gpsimd
        def _(pool):
            n = [0]

            def ch(ins):
                n[0] += 1
                ins.then_inc(s.pool_chain, 1)
                pool.wait_ge(s.pool_chain, n[0])

            def sel(ap, pattern, base, cm, fill=0.0, op=ALU.is_ge):
                ch(nc.gpsimd.affine_select(out=ap, in_=ap, compare_op=op, fill=fill, base=base,
                                           pattern=pattern, channel_multiplier=cm))

            pool.dma_start(ptab[:, :], t["page_table"].rearrange("(o b) n -> o (b n)", o=1)).then_inc(s.pagetab_loaded, 16)
            ch(nc.gpsimd.memset(cum[:, 0:384], 0.0))
            ch(nc.gpsimd.memset(cum[:, 384:1408], 1.0))
            sel(ut, [[1, P]], 0, -1)
            ch(nc.gpsimd.memset(ident[:, :], 0.0))
            sel(ident[:, :], [[-1, P]], 0, 1, 1.0, ALU.not_equal)
            ch(nc.gpsimd.memset(negq[:, :], 0.0))
            sel(negq[:, :], [[-1, P]], 0, 1, -BIG)
            ch(nc.gpsimd.memset(negT[:, :], 0.0))
            sel(negT[:, :], [[1, P]], 0, -1, -BIG)
            ch(nc.gpsimd.memset(lvl[:, :, :], 0.0))
            for l in range(7):
                b = 1 << l
                v = lvl[:, l, :].rearrange("p (n two b) -> p n two b", two=2, b=b)[:, :, 1, :]
                ch(nc.gpsimd.memset(v, 1.0))
                sel(v, [[-2 * b, P // (2 * b)], [0, b]], 0, 1)
                sel(v, [[2 * b, P // (2 * b)], [0, b]], b - 1, -1)
            m4d = msk[:, :, :].rearrange("p m (b q) -> p m b q", q=QS)
            ch(nc.gpsimd.memset(msk[:, 0:2, :], 1.0))
            ch(nc.gpsimd.memset(msk[:, 2:4, :], 0.0))
            ch(nc.gpsimd.memset(msk[:, 4, :], 1.0))
            for m, fill in ((0, 0.0), (1, 0.0), (2, -BIG), (3, -BIG)):
                sel(m4d[:, m], [[-QS, NB], [0, QS]], 0, 1, fill)
                sel(m4d[:, m], [[QS, NB], [0, QS]], QS - 1, -1, fill)
            sel(utS, [[1, TS]], 0, -1)
            sel(negTS, [[1, TS]], 0, -1, -BIG)
            sel(negQS, [[-1, TS]], 0, 1, -BIG)
            sel(bsel, [[-QS, NB]], 0, 1)
            sel(bsel, [[QS, NB]], QS - 1, -1)
            ch(nc.gpsimd.iota(iota[:, 0, :], pattern=[[1, C]], base=0, channel_multiplier=0,
                              allow_small_or_imprecise_dtypes=True))
            nc.gpsimd.iota(rev[:, :], pattern=[[-1, NE]], base=NE, channel_multiplier=0,
                           allow_small_or_imprecise_dtypes=True).then_inc(s.consts, 1)
            pool.wait_ge(s.pagetab_loaded, 16)
            cl = t["cache_logf"][0]
            for grp in range(2):
                with pool.Fori(0, 4) as bl:
                    for pg in range(NPAGE):
                        page = pool.value_load(ptab[0:1, bass.ds(bl * NPAGE + (grp * 32 + pg), 1)], min_val=0,
                                               max_val=cl.shape[0] - 1)
                        pool.dma_start(lfp[:, grp, pg, bass.ds(bl * 8, 8)],
                                       cl[bass.ds(page, 1)].rearrange("a r h -> r (a h)")).then_inc(s.bias_pages, 16)
            cvp = t["cache_v"][0]
            pool.wait_ge(s.proj_ps, 28)
            for b0, nb, free in ((0, 2, None), (2, NB - 2, s.vpage_free)):
                with pool.Fori(0, nb // 2) as bb:
                    for n in range(16):
                        page = pool.value_load(ptab[0:1, bass.ds(bb * 16 + (b0 * NPAGE + n), 1)], min_val=0,
                                               max_val=cvp.shape[0] - 1)
                        if free is not None:
                            pool.wait_ge(free, bb * 16 + (n + 1))
                        pool.dma_start(vring[:, n, :], cvp[bass.ds(page, 1)]
                                       .rearrange("a r h d -> r (a h d)")).then_inc(s_v[n // 4], 16)

        @block.tensor
        def _(pe):
            mm = nc.tensor.matmul
            tr = nc.tensor.transpose

            def transpose_h(n):
                pe.wait_ge(s.h_ready, 3 * (n + 1))
                for k in range(KD):
                    if k >= 4:
                        pe.wait_ge(s.hT_done, KD * n + k - 3)
                    for i, (r0, m) in enumerate(TOK):
                        last = tr(ps[:, k % 4, r0:r0 + m], htok[0:m, i, k::KD], ident[0:m, 0:m])
                    last.then_inc(s.hT_ps, 1)
                pe.wait_ge(s.hT_done, KD * (n + 1))

            def out_proj(part):
                for j in part:
                    wait_unit(pe, 14 + j)
                    w = cview(14 + j)
                    for c in range(2):
                        for i, (r0, m) in enumerate(TOK):
                            for hf in range(2):
                                last = mm(ps[0:m, 2 * i + hf, :], mixT[:, 2 * j + c, r0:r0 + m],
                                          w[:, c, 512 * hf:512 * (hf + 1)],
                                          start=(j == 0 and c == 0), stop=(j == 3 and c == 1))
                    last.then_inc(s.w_used, 1)

            pe.wait_ge(s.consts, 1)
            transpose_h(0)
            pe.wait_ge(s.small_loaded, 16 * SMALL)
            for i, (r0, m) in enumerate(TOK):
                for k in range(KD):
                    last = mm(ps[0:m, 4, 16 * i:16 * i + 16], hT[:, k, r0:r0 + m], wsm[:, k, :],
                              start=k == 0, stop=k == KD - 1)
            last.then_inc(s.fz_ps, 1)
            tr(ps[:, 6, 0:48], cwr[0:48, :], ident[0:48, 0:48]).then_inc(s.cw_ps, 1)
            for c in range(NCT):
                last = tr(ps[:, 5, 24 * c:24 * (c + 1)], scin[0:24, P * c:P * (c + 1)], ident[0:24, 0:24])
            last.then_inc(s.cs_ps, 1)
            for c in range(28):
                if c % 2 == 0:
                    wait_unit(pe, c // 2)
                if c >= 4:
                    pe.wait_ge(s.proj_done, c - 3)
                w = kview(c // 2)
                for k in range(KD):
                    last = mm(ps[:, c % 4, 0:T], w[:, k, P * (c % 2):P * (c % 2 + 1)], hT[:, k, :],
                              start=k == 0, stop=k == KD - 1)
                last.then_inc(s.proj_ps, 1)
            pe.wait_ge(s.proj_done, 28)
            for j in range(6):
                i, (r0, m) = j // 2, TOK[j // 2]
                if j >= 3:
                    pe.wait_ge(s.kv_copied, j - 2)
                for c in range(4):
                    src = qkT[:, 4 + c, r0:r0 + m] if j % 2 == 0 else vT[:, c, r0:r0 + m]
                    last = tr(ps[0:m, j % 3, P * c:P * (c + 1)], src, ident[:, :])
                last.then_inc(s.kv_ps, 1)
            pe.wait_ge(s.cs27, 2)
            pe.wait_ge(s.cs_copied, 1)
            pe.wait_ge(s.cw_done, 1)
            for c in range(NCT):
                last = tr(ps[0:27, 5 + c // 4, P * (c % 4):P * (c % 4 + 1)], cs27[:, c, :], ident[:, :])
            last.then_inc(s.cst_ps, 1)
            pe.wait_ge(s.neglogf, 1)
            pe.wait_ge(s.kv_copied, 6)

            def pa_scores(h):
                pr, o = h // 2, 64 * (h % 2)
                b = ps[:, h % 2, :]
                if h >= 2:
                    pe.wait_ge(s.pa_exp, 2 * (h - 1))
                    pe.wait_ge(s.pa_max, 2 * (h - 1))
                for qb, c0, nk in ((0, 0, P), (1, P, TP)):
                    mm(b[:, c0:c0 + nk], qkT[o:o + 64, pr, P * qb:P * (qb + 1)], qkT[o:o + 64, 4 + pr, 0:nk],
                       start=True, stop=False, skip_group_check=True)
                    mm(b[:, c0:c0 + nk], bc(nlf[:, 0, h:h + 1], [P, P]), cum[:, 384:384 + nk],
                       start=False, stop=False, skip_group_check=True)
                    if qb:
                        mm(b[:, c0 + P:c0 + nk], bc(nlf[:, 1, h:h + 1], [P, P]), ut,
                           start=False, stop=False, skip_group_check=True)
                    last = mm(b[:, c0 + nk - P:c0 + nk], ident[:, :], negq[:, :], start=False, stop=True,
                              skip_group_check=True)
                last.then_inc(s.pa_s_ps, 1)

            def pa_out(h):
                pr = h // 2
                pe.wait_ge(s.pa_p, 2 * (h + 1))
                if h == 1:
                    pe.wait_ge(s.cst_done, 1)
                if h >= 2:
                    pe.wait_ge(s.pa_pt, h - 1)
                for j in range(3):
                    last = tr(ps[:, 2 + h % 2, P * j:P * (j + 1)], pP[:, h % 2, P * j:P * (j + 1)], ident[:, :])
                last.then_inc(s.pa_pt_ps, 1)
                pe.wait_ge(s.pa_pt, h + 1)
                if h >= 2:
                    pe.wait_ge(s.pa_o, h - 1)
                b = ps[:, 4 + h % 2, :]
                mm(b[:, 0:TP], vtok[:, 0, P * pr:P * (pr + 1)], pPT[:, h % 2, 0:TP], start=True, stop=False,
                   skip_group_check=True)
                mm(b[:, P:TP], vtok[:, 1, P * pr:P * (pr + 1)], pPT[:, h % 2, TP:384], start=False, stop=True,
                   skip_group_check=True).then_inc(s.pa_o_ps, 1)

            for h in range(HA + 1):
                if h < HA:
                    pa_scores(h)
                if h:
                    pa_out(h - 1)
            pe.wait_ge(s.pa_o, HA)
            pe.wait_ge(s.qz_ready, 1)

            def k_transpose(n):
                pe.wait_ge(s_k[n % 4], 16 * (n // 4 + 1))
                if n >= 2:
                    pe.wait_ge(s.kt_done, n - 1)
                for c in range(NPAIR):
                    last = tr(ps[:, 3 + n % 2, P * c:P * (c + 1)], kring[:, n % 4, P * c:P * (c + 1)], ident[:, :])
                last.then_inc(s.kt_ps, 1)

            pe.wait_ge(s.dl_sq, 1)
            for j in range(8):
                if j >= 3:
                    pe.wait_ge(s.dl_rms, j - 2)
                mm(ps[:, 5 + j % 3, 0:T], one, dsq[:, j, :], start=True, stop=True).then_inc(s.dl_ss_ps, 1)
            for grp in range(2):
                pe.wait_ge(s.ks_done, grp + 1)
                if grp:
                    pe.wait_ge(s.sa_exp, 1)
                for hf in range(2):
                    mm(ps[:, hf, :], ident[:, :], zero512, start=True, stop=False, skip_group_check=True)
                for pg in range(NPAGE):
                    b = ps[:, pg // 4, P * (pg % 4):P * (pg % 4 + 1)]
                    mm(b, lfx[:, pg, :], ut, start=False, stop=False, skip_group_check=True)
                    if pg:
                        mm(b, acx[:, pg - 1, :], one, start=False, stop=False,
                           skip_group_check=True)
                mm(ps[:, 2, 0:TS], acx[:, NPAGE - 1, :], one[:, 0:TS], start=True, stop=False,
                   skip_group_check=True)
                mm(ps[:, 2, 0:TS], lfn[0:TS, :], utS, start=False, stop=False, skip_group_check=True)
                mm(ps[:, 2, 0:TS], eg[0:TS, grp, :], negQS, start=False, stop=False, skip_group_check=True)
                k_transpose(32 * grp)
                for n in range(32 * grp, 32 * grp + 32):
                    if n < 32 * grp + 31:
                        k_transpose(n + 1)
                    b, pg = n // NPAGE, n % NPAGE
                    pe.wait_ge(s.kt_done, n + 1)
                    for c in range(NPAIR):
                        last = mm(ps[:, pg // 4, P * (pg % 4):P * (pg % 4 + 1)], qz[:, NPAIR * b + c, :],
                                  kpT[:, n % 2, c, :], start=False, stop=False, skip_group_check=True)
                    last.then_inc(s.kpage_free, 1)
                for b in range(4 * grp, 4 * grp + 4):
                    for c in range(NPAIR):
                        last = mm(ps[:, 2, 0:TS], qz[:, NPAIR * b + c, :], qkT[:, 4 + c, TP:T],
                                  start=False, stop=(b % 4 == 3 and c == 3), skip_group_check=True)
                last.then_inc(s.sa_s_ps, 1)
                pe.wait_ge(s.sa_p, grp + 1)
                if grp:
                    pe.wait_ge(s.sa_o, 3)
                else:
                    pe.wait_ge(s.dl_rms, 8)
                for j in range(9):
                    m = P if j < 8 else TS
                    if j == 8:
                        last = tr(ps[0:TS, 7, 0:P], sS[:, 1024:1056], ident[:, :])
                    else:
                        last = tr(ps[:, 5 + j // 4, P * (j % 4):P * (j % 4 + 1)], sS[:, P * j:P * (j + 1)], ident[:, :])
                last.then_inc(s.sa_pt_ps, 1)
                pe.wait_ge(s.sa_pt, grp + 1)
                mm(ps[:, 7, :], ident[:, :], zero512, start=True, stop=False, skip_group_check=True)
                for n in range(32):
                    bl, pg = n // NPAGE, n % NPAGE
                    g = 32 * grp + n
                    if n % 4 == 0:
                        pe.wait_ge(s_v[(g // 4) % 4], 64 * (g // 16 + 1))
                    mm(ps[32 * bl:32 * bl + 32, 7, :], sPT[:, pg, 32 * bl:32 * bl + 32], vring[:, g % 16, :],
                       start=False, stop=False, skip_group_check=True).then_inc(s.vpage_free, 1)
                for bl in range(4):
                    last = mm(ps[32 * bl:32 * bl + 32, 7, :], sPT[0:TS, 8, 32 * bl:32 * bl + 32], vtok[0:TS, 2, :],
                              start=False, stop=True, skip_group_check=True)
                last.then_inc(s.sa_o_ps, 1)
                pe.wait_ge(s.sa_o, 3 * grp + 1)
                for c in range(NPAIR):
                    last = tr(ps[:, 5, P * c:P * (c + 1)], sO[:, P * c:P * (c + 1)], ident[:, :])
                last.then_inc(s.sa_o_ps, 1)
            pe.wait_ge(s.sa_o, 6)
            pe.wait_ge(s.dl_qk, 8)
            for j in range(6):
                i, (r0, m) = j // 2, TOK[j // 2]
                if j >= 3:
                    pe.wait_ge(s.dl_tok, j - 2)
                for c in range(4):
                    last = tr(ps[0:m, j % 3, P * c:P * (c + 1)], cv[:, (4 if j % 2 == 0 else 8) + c, r0:r0 + m],
                              ident[:, :])
                last.then_inc(s.dl_tok_ps, 1)
            for i in range(3):
                m = TOK[i][1]
                tri = ut if i < 2 else utS
                for h in range(HB):
                    last = mm(ps[:, 3 + i, P * h:P * h + m], bc(gg[0:m, i, h:h + 1], [m, P]), tri,
                              start=True, stop=True)
                last.then_inc(s.dl_R_ps, 1)
            for i in range(3):
                m = TOK[i][1]
                mm(ps[0:m, 6, 4 * i:4 * i + 4], ut if i < 2 else utS, gg[0:m, i, :], start=True, stop=True)
                last = mm(ps[0:m, 6, 16 + 4 * i:20 + 4 * i], one if i < 2 else same, gg[0:m, i, :], start=True,
                          stop=True)
            last.then_inc(s.dl_cols_ps, 1)
            pe.wait_ge(s.dl_tok, 6)
            for i, (r0, m) in enumerate(TOK):
                if i:
                    pe.wait_ge(s.dl_kk, 2 * i)
                for w in range(2):
                    for h in range(HB):
                        last = mm(ps[0:m, w, P * h:P * h + m], cv[:, 4 + h, r0:r0 + m],
                                  cv[:, (4 if w == 0 else 0) + h, r0:r0 + m], start=True, stop=True)
                last.then_inc(s.dl_kk_ps, 1)
            pe.wait_ge(s.dl_kk, 6)
            pe.wait_ge(s.dl_eR, 3)
            pe.wait_ge(s.dl_dt, 12)
            for l in range(7):
                for i in inv_tiles(l):
                    pe.wait_ge(s.dl_mt, inv_no(l, i))
                    pe.wait_ge(s.dl_t, 1 + (2 * inv_no(l - 1, i) if l else 0))
                    u = inv_ps(i, 0)
                    m = TOK[i][1]
                    for h in range(HB):
                        last = mm(u[:, h, :], dMT[0:m, i, h, 0:m], dT[0:m, i, h, 0:m], start=True, stop=True)
                    last.then_inc(s.dl_u_ps, 1)
                for i in inv_tiles(l):
                    m = TOK[i][1]
                    pe.wait_ge(s.dl_u, inv_no(l, i))
                    for h in range(HB):
                        mm(inv_ps(i, 1)[:, h, :], dTT[0:m, i, h, 0:m], dU[0:m, i, h, 0:m], start=True, stop=True)
                    for h in range(HB):
                        last = mm(inv_ps(i, 2)[:, h, :], dU[0:m, i, h, 0:m], dTT[0:m, i, h, 0:m],
                                  start=True, stop=True)
                    last.then_inc(s.dl_t_ps, 1)
            pe.wait_ge(s.dl_scaled, 2)
            pe.wait_ge(s.dl_t, 1 + 2 * inv_no(6, 1))
            for i, (r0, m) in enumerate(TOK):
                if i:
                    pe.wait_ge(s.dl_w, 2 * i)
                for h in range(HB):
                    mm(ps[0:m, 0, P * h:P * (h + 1)], dTT[0:m, i, h, 0:m], vb[0:m, i, h, :], start=True, stop=True)
                for h in range(HB):
                    last = mm(ps[:, 1, P * h:P * h + m], kbe[0:m, i, h, :], dTT[0:m, i, h, 0:m], start=True, stop=True)
                last.then_inc(s.dl_w_ps, 1)
            pe.wait_ge(s.dl_w, 6)
            pe.wait_ge(s.dl_qdec, 1)
            for h in range(HB):
                last = mm(ps[:, 2, P * h:P * (h + 1)], kdt[:, 0, h, :], wv[:, 0, h, :], start=True, stop=True)
            last.then_inc(s.dl_s_ps, 1)
            pe.wait_ge(s.dl_s, 1)
            for h in range(HB):
                last = mm(ps[:, 3, P * h:P * (h + 1)], wkT[:, 1, h, :], Sp[:, 0, h, :], start=True, stop=True)
            last.then_inc(s.dl_v1_ps, 1)
            pe.wait_ge(s.dl_v1, 1)
            for h in range(HB):
                last = mm(ps[:, 2, P * h:P * (h + 1)], kdt[:, 1, h, :], wv[:, 1, h, :], start=True, stop=True)
            last.then_inc(s.dl_s_ps, 1)
            pe.wait_ge(s.s0_loaded, 16)
            for h in range(HB):
                for b in range(NB):
                    last = mm(ps[:, 4, TS * h + QS * b:TS * h + QS * (b + 1)], S0[:, HB * b + h, :],
                              wkT[:, 2, h, QS * b:QS * (b + 1)], start=True, stop=True)
            last.then_inc(s.dl_vs_ps, 1)
            pe.wait_ge(s.dl_vsT, 1)
            for h in range(HB):
                last = tr(ps[0:TS, 5, P * h:P * (h + 1)], vsT[:, TS * h:TS * (h + 1)], ident[:, :])
            last.then_inc(s.dl_vt_ps, 1)
            pe.wait_ge(s.dl_vs, 1)
            for h in range(HB):
                b = ps[:, 6 + h % 2, :]
                if h >= 2:
                    pe.wait_ge(s.dl_o, h - 1)
                for i, (r0, m) in enumerate(TOK):
                    mm(b[:, r0:r0 + m], wv[0:m, i, h, :], dQK[0:m, i, h, 0:m], start=(i == 0), stop=False,
                       skip_group_check=True)
                mm(b[:, P:TP], Sp[:, 0, h, :], cv[:, h, P:TP], start=False, stop=False, skip_group_check=True)
                for q in range(NB):
                    last = mm(b[:, TP + QS * q:TP + QS * (q + 1)], S0[:, HB * q + h, :],
                              cv[:, h, TP + QS * q:TP + QS * (q + 1)], start=False, stop=q == NB - 1,
                              skip_group_check=True)
                last.then_inc(s.dl_o_ps, 1)
            pe.wait_ge(s.dl_st_out, 1)
            out_proj((0,))
            pe.wait_ge(s.dl_osq, 1)
            for h in range(HB):
                if h >= 2:
                    pe.wait_ge(s.dl_orms, h - 1)
                mm(ps[:, 6 + h % 2, 0:T], one, osq[:, h, :], start=True, stop=True).then_inc(s.dl_oss_ps, 1)
            out_proj((1,))
            pe.wait_ge(s.dl_vexp, NB)
            pe.wait_ge(s.dl_orms, HB)
            vx = vexp.rearrange("p b (h e) -> p b h e", h=HB)
            for j in range(8):
                h, q = j // 2, j % 2
                if j >= 2:
                    pe.wait_ge(s.dl_su, j - 1)
                mm(ps[:, 6 + j % 2, :], kdt[0:TS, 2, h, :], vx[0:TS, 4 * q:4 * q + 4, h, :], start=True,
                   stop=True).then_inc(s.dl_su_ps, 1)
            pe.wait_ge(s.dl_mixed, HB)
            pe.wait_ge(s.dl_su, 8)
            pe.wait_ge(s.dl_o, HB)
            out_proj((2, 3))

            def moe(layer, n):
                transpose_h(n)
                pe.wait_ge(s.rest_loaded, 16 * REST)
                for i, (r0, m) in enumerate(TOK):
                    for k in range(KD):
                        last = mm(ps[0:m, 4, 36 * i:36 * i + 36], hT[:, k, r0:r0 + m], wr[:, layer, k, :],
                                  start=k == 0, stop=k == KD - 1)
                last.then_inc(s.rl_ps, 1)
                pe.wait_ge(s.rt_oh, layer + 1)
                for i, (r0, m) in enumerate(TOK):
                    for j in range(i + 1):
                        n_ = TOK[j][1]
                        last = mm(ps[0:m, 5, 4 * i:4 * i + 4], (ut if j == i else one)[0:n_, 0:m], oh4[0:n_, j, :],
                                  start=j == 0, stop=j == i)
                for j in range(3):
                    n_ = TOK[j][1]
                    last = mm(ps[0:1, 5, 16:20], one[0:n_, 0:1], oh4[0:n_, j, :], start=j == 0, stop=j == 2)
                last.then_inc(s.rank_ps, 1)
                def iteration(li):
                    it = li + layer * ITERS
                    pe.wait_ge(s.perm_ready, 3 * (it + layer) + 3)
                    pe.wait_ge(s.xadd, it * 6)
                    for k in range(KD):
                        for i, (r0, m) in enumerate(TOK):
                            last = mm(ps[:, k // 4, C * (k % 4):C * (k % 4 + 1)], htok[:, i, k::KD], pm[:, i, :],
                                      start=i == 0, stop=i == 2)
                    last.then_inc(s.hg_ps, 1)
                    pe.wait_ge(s.rank_done, layer + 1)
                    for i in range(3):
                        mm(ps[0:C, 4, GCOL:GCOL + EG], pm[:, i, :], g8[:, i, :], start=i == 0, stop=i == 2)
                    for i, (r0, m) in enumerate(TOK):
                        last = tr(ps[0:C, 4, r0:r0 + P], pm[:, i, :], ident[:, :])
                    last.then_inc(s.pt_ps, 1)
                    pe.wait_ge(s.hg_done, 2 * it + 2)

                    def down(e):
                        u = MOE0[layer] + 3 * e + 2
                        wait_unit(pe, u, li)
                        pe.wait_ge(s.act_done, it * EG + e + 1)
                        if e == 0:
                            pe.wait_ge(s.pt_done, it + 1)
                        w = cview(u)
                        for f in range(FT):
                            for hf in range(2):
                                last = mm(ps[0:C, 4 + hf, :], av[:, e % 2, f, :], w[:, f, 512 * hf:512 * (hf + 1)],
                                          start=(e == 0 and f == 0), stop=(e == EG - 1 and f == FT - 1))
                        last.then_inc(s.dn_used, 1)

                    for e in range(EG):
                        if e >= 2:
                            pe.wait_ge(s.act_done, it * EG + e - 1)
                        b = ps[:, 2 + e % 2, 0:4 * C].rearrange("p (a f c) -> p a f c", a=2, f=FT)
                        for a in range(2):
                            u = MOE0[layer] + 3 * e + a
                            wait_unit(pe, u, li)
                            w = kview(u)
                            for f in range(FT):
                                for k in range(KD):
                                    last = mm(b[:, a, f, :], w[:, k, f::FT], hg[:, k, :], start=k == 0,
                                              stop=k == KD - 1)
                            last.then_inc((s.g_used, s.gu_ps)[a], 1)
                        if e == 0:
                            pe.wait_ge(s.xadd, XADD0 + it * 6)
                            pe.wait_ge(s.moe_chain, it * (EG + 2) + 1)
                            for hf in range(2):
                                last = mm(ps[:, 6 + hf, 0:4 * C], one[0:C, :], dg[0:C, 4 * hf:4 * hf + 4, :],
                                          start=True, stop=True)
                            last.then_inc(s.gs_ps, 1)
                        else:
                            down(e - 1)
                    down(EG - 1)
                    pe.wait_ge(s.ysb_done, 2 * it + 2)
                    pe.wait_ge(s.gs_done, 2 * it + 2)
                    for j in range(6):
                        i, (r0, m) = j // 2, TOK[j // 2]
                        if j >= 4:
                            pe.wait_ge(s.xadd, XADD0 + it * 6 + j - 3)
                        mm(ps[0:m, (6, 7, 0, 1)[j % 4], :], pmT[0:C, r0:r0 + m], ysb[0:C, 512 * (j % 2):512 * (j % 2 + 1)],
                           start=True, stop=True).then_inc(s.sc_ps, 1)

                with pe.Fori(0, NG) as li:
                    iteration(li)
                with pe.If(more(pe, layer) > 0):
                    with pe.Fori(NG, ITERS) as li:
                        iteration(li)
                with pe.Else():
                    skip_rounds(pe, layer, (s.hg_ps, 1), (s.gs_ps, 1), (s.pt_ps, 1), (s.g_used, EG), (s.gu_ps, EG),
                                (s.dn_used, EG), (s.sc_ps, 6))
            moe(0, 1)
            pe.wait_ge(s.xadd, XADD0 + 6 * ITERS)
            transpose_h(2)
            for c in range(NU + 2):
                if c < NU:
                    if c % 2 == 0:
                        wait_unit(pe, ODD0 + c // 2)
                    if c >= 4:
                        pe.wait_ge(s.gm_v, v_chan(c - 4))
                    for k in range(KD):
                        last = mm(ps[:, c % 4, 0:T], kview(ODD0 + c // 2)[:, k, P * (c % 2):P * (c % 2 + 1)],
                                  hT[:, k, :], start=k == 0, stop=k == KD - 1)
                    last.then_inc(s.gm_v_ps, 1)
                if c >= 2:
                    pe.wait_ge(s.gm_v, max(v_chan(c - 2), v_rows(c - 4) if c >= 4 else 0))
                    for i, (r0, m) in enumerate(TOK):
                        last = tr(ps[0:m, 4 + c % 2, P * i:P * (i + 1)], vg[:, (c - 2) % 4, r0:r0 + m], ident[:, :])
                    last.then_inc(s.gm_v_ps, 1)
            pe.wait_ge(s.ws_loaded, 64)
            for h in range(HC):
                if h == 4:
                    pe.wait_ge(s.ws_done, 4)
                last = tr(ps[:, 6, P * (h % 4):P * (h % 4 + 1)], wsn[:, h, :], ident[:, :])
                last.then_inc(s.ws_ps, 1)
            pe.wait_ge(s.ws_done, 9)
            mm(ps[0:TS, 7, 0:HC * QS], rep[0:QS, :, :], wmT[0:QS, :, 0:QS], start=True,
               stop=True).then_inc(s.wrep_ps, 1)
            pe.wait_ge(s.gm_v, 2 * NU)
            for c in range(NU):
                u = ODD0 + 8 + c // 2
                if c % 2 == 0:
                    wait_unit(pe, u)
                if c >= 4:
                    pe.wait_ge(s.gm_u, c - 3)
                for k in range(KD):
                    last = mm(ps[:, c % 4, 0:T], kview(u)[:, k, P * (c % 2):P * (c % 2 + 1)], hT[:, k, :],
                              start=k == 0, stop=k == KD - 1)
                last.then_inc(s.gm_u_ps, 1)
            pe.wait_ge(s.gm_vn, 3)
            pe.wait_ge(s.gm_bias, 1)
            pe.wait_ge(s.wrep_done, HC)
            pe.wait_ge(s.gm_u, NU)
            for c in range(NU):
                h = c // 2
                b = ps[:, c % 4, :]
                if c >= 4:
                    pe.wait_ge(s.gm_m, c - 3)
                mm(b[:, 0:T], cum[0:1, 512:640], bsr[0:1, h, :], start=True, stop=False, skip_group_check=True)
                for i, (r0, m) in enumerate(TOK):
                    last = mm(b[:, r0:r0 + m], vrow[0:m, i, P * c:P * (c + 1)],
                              wmT[:, h, :] if i < 2 else wS[0:TS, h, :], start=False, stop=i == 2,
                              skip_group_check=True)
                last.then_inc(s.gm_m_ps, 1)
            pe.wait_ge(s.gm_m, NU)
            for j in range(8):
                wait_unit(pe, ODD0 + 16 + j)
                w = cview(ODD0 + 16 + j)
                for dt, c in ([(dt, c) for c in range(2) for dt in range(8)] if j < 7 else
                              [(dt, c) for dt in range(8) for c in range(2)]):
                    last = mm(ps[:, dt, 0:T], w[:, c, P * dt:P * (dt + 1)], uT[:, 2 * j + c, :],
                              start=(j == 0 and c == 0), stop=(j == 7 and c == 1))
                    if j == 7 and c == 1 and dt < 7:
                        last.then_inc(s.gm_m_ps, 1)
                if j < 7:
                    last.then_inc(s.w_used, 1)
            last.then_inc(s.gm_m_ps, 1)
            for dt in range(8):
                pe.wait_ge(s.gm_u, NU + dt + 1)
                for i, (r0, m) in enumerate(TOK):
                    last = tr(ps[0:m, dt, P * i:P * (i + 1)], hT[:, dt, r0:r0 + m], ident[:, :])
                last.then_inc(s.gm_m_ps, 1)
            moe(1, 3)

        @block.scalar
        def _(act):
            n = [0]
            A_ = nc.scalar.activation

            def ch(ins):
                n[0] += 1
                ins.then_inc(s.act_chain, 1)
                act.wait_ge(s.act_chain, n[0])

            sl = []
            sl.append((nw[:, 0, :], t["norm_mix"][0].rearrange("(p k) -> p k", k=KD)))
            sl.append((wsm[:, :, 0:8], w_in[:, :, 1536:1544]))
            sl.append((wsm[:, :, 8:16], w_in[:, :, 3080:3088]))
            sl.append((biasrow[:, 0:8], t["fox_forget_bias"][0:1, :].partition_broadcast(P)))
            sl.append((biasrow[:, 8:12], t["dn_dt_bias"][0:1, :].partition_broadcast(P)))
            sl.append((alog, t["dn_a_log"][0:1, :].partition_broadcast(P)))
            sl.append((onw, t["dn_norm_w"][0].rearrange("(p o) -> p o", o=1)))
            sl.append((cwr[0:48, :], t["dn_conv_w"][0].rearrange("w (c p) -> (w c) p", p=P)))
            sl.append((scin[0:24, :], t["state_conv"][0].rearrange("b w c -> (b w) c")))
            assert len(sl) == SMALL
            sl.append((nw[:, 1, :], t["norm_ffn"][0].rearrange("(p k) -> p k", k=KD)))
            sl.append((nw[:, 2, :], t["norm_mix"][1].rearrange("(p k) -> p k", k=KD)))
            sl.append((nw[:, 3, :], t["norm_ffn"][1].rearrange("(p k) -> p k", k=KD)))
            for l in range(2):
                sl.append((wr[:, l, :, 0:NG], t["moe_router_group"][l].rearrange("(p k) g -> p k g", k=KD)))
                sl.append((wr[:, l, :, NG:NG + NE], t["moe_router_expert"][l].rearrange("(p k) g -> p k g", k=KD)))
            for i, (dst, src) in enumerate(sl):
                act.dma_start(dst, src).then_inc(s.small_loaded if i < SMALL else s.rest_loaded, 16)

            def norm_stats(n_):
                for i, (r0, m) in enumerate(TOK):
                    if n_:
                        act.wait_ge(s.x_new, 3 * (n_ - 1) + i + 1)
                    A_(htok[0:m, i, :], x[0:m, i, :], ACT.Square,
                       accum_out=ss[0:m, 3 * n_ + i:3 * n_ + i + 1]).then_inc(s.ss_done, 1)
                act.wait_ge(s.ss_done, 3 * (n_ + 1))
                A_(rms[:, 3 * n_:3 * n_ + 3], ss[:, 3 * n_:3 * n_ + 3], ACT.Sqrt, scale=1.0 / D,
                   bias=epsb).then_inc(s.rms_done, 1)

            act.wait_ge(s.x_loaded, 48)
            act.wait_ge(s.fz_sig, 1)
            norm_stats(0)
            act.wait_ge(s.fz_abs, 1)
            ch(A_(fa, fa, ACT.Exp, scale=-1.0))
            ch(A_(expa, alog, ACT.Exp))
            ch(A_(fz1.rearrange("p (t c) -> p t c", t=3)[:, :, 0:4], fz3[:, :, 12:16], ACT.Exp, scale=-1.0))
            A_(fb, fa, ACT.Ln, bias=1.0).then_inc(s.fz_ln, 1)

            def silu_conv(c):
                act.wait_ge(s.conv_raw, c + 1)
                A_(cv[:, c, 0:TP], craw[:, c, 0:TP], ACT.Silu)
                A_(cv[:, c, TP:T].rearrange("p (b w) -> p b w", b=NB),
                   craw[:, c, XS:XS + NB * 7].rearrange("p (b w) -> p b w", b=NB)[:, :, 0:4],
                   ACT.Silu).then_inc(s.conv_done, 1)

            for c in range(28):
                act.wait_ge(s.proj_ps, c + 1)
                b = ps[:, c % 4, :]
                if c < 12:
                    A_(xc[:, c, 3:XS], b[:, 0:TP], ACT.Copy)
                    A_(xc[:, c, XS:XC].rearrange("p (b w) -> p b w", b=NB)[:, :, 3:7],
                       b[:, TP:T].rearrange("p (b w) -> p b w", b=NB), ACT.Copy).then_inc(s.proj_done, 1)
                elif c < 16:
                    A_(gT[:, c - 12, :], b[:, 0:T], ACT.Silu).then_inc(s.proj_done, 1)
                elif c < 24:
                    A_(qkT[:, c - 16, :], b[:, 0:T], ACT.Copy, scale=DA ** -0.5 if c < 20 else 1.0)\
                        .then_inc(s.proj_done, 1)
                else:
                    A_(vT[:, c - 24, :], b[:, 0:T], ACT.Copy).then_inc(s.proj_done, 1)
                if 2 <= c < 14:
                    silu_conv(c - 2)
                if c == 14:
                    act.wait_ge(s.proj_done, NCT)
                    A_(cs27[:, :, 0:24].rearrange("p c (b w) -> p c b w", b=NB),
                       xc[:, :, XS:XC].rearrange("p c (b w) -> p c b w", b=NB)[:, :, :, 4:7], ACT.Copy)\
                        .then_inc(s.cs27, 1)
                    A_(cs27[:, :, 24:27], xc[:, :, TP:TP + 3], ACT.Copy).then_inc(s.cs27, 1)
            act.wait_ge(s.conv_done, NCT)
            A_(dsq[:, :, :], cv[:, 0:8, :], ACT.Square).then_inc(s.dl_sq, 1)
            act.wait_ge(s.kv_copied, 6)
            for i, (r0, m) in enumerate(TOK):
                for nm, src in (("k", ktok), ("v", vtok)):
                    if i < 2:
                        dst = t[nm + "_prompt"][0, 0, r0:r0 + m].rearrange("l h d -> l (h d)")
                    else:
                        dst = t[nm + "_sample"][0].rearrange("b l h d -> (b l) (h d)")
                    act.dma_start(dst, src[0:m, i, :]).then_inc(s.out_misc, 16)
            for i, (r0, m) in enumerate(TOK):
                dst = t["logf_prompt"][0, 0, r0:r0 + m] if i < 2 else t["logf_sample"][0].rearrange("b l h -> (b l) h")
                act.dma_start(dst, lf[0:m, i, :]).then_inc(s.out_misc, 16)
            for h in range(HA):
                b = ps[:, h % 2, :]
                if h >= 2:
                    act.wait_ge(s.pa_pt_ps, h - 1)
                for qb, c0, nk in ((0, 0, P), (1, P, TP)):
                    j = 2 * h + qb
                    act.wait_ge(s.pa_max, 2 * h + 2)
                    A_(pP[:, h % 2, c0:c0 + nk], b[:, c0:c0 + nk], ACT.Exp, bias=pmax[:, j:j + 1],
                       accum_out=psm[:, j:j + 1]).then_inc(s.pa_exp, 1)
                act.wait_ge(s.pa_pt_ps, h + 1)
                A_(pPT[:, h % 2, :], ps[:, 2 + h % 2, 0:384], ACT.Copy).then_inc(s.pa_pt, 1)
            act.wait_ge(s.cst_done, 1)
            act.dma_start(t["conv_sample"][0].rearrange("b w c -> (b w) c"), cst[0:24, :]).then_inc(s.out_misc, 16)
            act.dma_start(t["conv_prompt"][0, 0], cst[24:27, :]).then_inc(s.out_misc, 16)
            for j in range(8):
                act.wait_ge(s.dl_ss_ps, j + 1)
                A_(dsq[:, j, :], ps[:, 5 + j % 3, 0:T], ACT.Sqrt, scale=float(DB) if j < 4 else 1.0,
                   bias=epsq if j < 4 else epsb).then_inc(s.dl_rms, 1)
            for grp in range(2):
                for m in range(32 * grp, 32 * grp + 32):
                    act.wait_ge(s.kt_ps, m + 1)
                    if m >= 2:
                        act.wait_ge(s.kpage_free, 4 + m - 1)
                    A_(kpT[:, m % 2], ps[:, 3 + m % 2, :].rearrange("p (c k) -> p c k", c=NPAIR),
                       ACT.Copy).then_inc(s.kt_done, 1)
                act.wait_ge(s.sa_max, grp + 1)
                A_(sS[:, 0:1056], ps[:, 0:3, :].rearrange("p a b -> p (a b)")[:, 0:1056], ACT.Exp, bias=pmax[:, 16 + grp:17 + grp],
                   accum_out=psm[:, 16 + grp:17 + grp]).then_inc(s.sa_exp, 1)
                act.wait_ge(s.sa_pt_ps, grp + 1)
                ch(A_(sPT[:, 0:8, :], ps[:, 5:7, :].rearrange("p a (b c) -> p (a b) c", c=P), ACT.Copy))
                A_(sPT[0:TS, 8, :], ps[0:TS, 7, 0:P], ACT.Copy).then_inc(s.sa_pt, 1)
            for i in range(3):
                m = TOK[i][1]
                act.wait_ge(s.dl_R_ps, i + 1)
                src = ps[:, 3 + i, :].rearrange("p (h c) -> p h c", h=HB)[:, :, 0:m]
                A_(eR[:, i, :, 0:m], src, ACT.Exp).then_inc(s.dl_eR, 1)
            act.wait_ge(s.dl_cols, 1)
            ch(A_(egc, gcc, ACT.Exp))
            A_(kdc, kdc, ACT.Exp).then_inc(s.dl_cols, 1)
            for i in range(3):
                m = TOK[i][1]
                act.wait_ge(s.dl_dt, 4 * (i + 1))
                A_(dDT[0:m, i, :, 0:m], dDT[0:m, i, :, 0:m], ACT.Exp).then_inc(s.dl_dtx, 1)
            for h in range(HB):
                act.wait_ge(s.dl_o_ps, h + 1)
                A_(oT[:, h, :], ps[:, 6 + h % 2, 0:T], ACT.Copy).then_inc(s.dl_o, 1)
            act.wait_ge(s.dl_o, HB)
            A_(osq[:, :, :], oT[:, :, :], ACT.Square).then_inc(s.dl_osq, 1)
            for h in range(HB):
                act.wait_ge(s.dl_oss_ps, h + 1)
                A_(osq[:, h, :], ps[:, 6 + h % 2, 0:T], ACT.Sqrt, scale=1.0 / DB, bias=epsb).then_inc(s.dl_orms, 1)
            act.wait_ge(s.dl_st_out, 1)
            act.dma_start(t["delta_prompt"][0, 0].rearrange("h k v -> k h v"), Sp[:, 1]).then_inc(s.out_misc, 16)
            act.wait_ge(s.dl_su, 8)
            act.dma_start(t["delta_sample"][0].rearrange("b h k v -> k (b h) v"), S0[:, :, :]).then_inc(s.out_misc, 16)

            def moe(layer, n_):
                norm_stats(n_)
                act.wait_ge(s.rt_e4x, 2 * layer + 1)
                A_(e4, d4, ACT.Exp).then_inc(s.rt_exp2, 1)
                act.wait_ge(s.rt_e4x, 2 * layer + 2)
                A_(ex2, ex2, ACT.Exp).then_inc(s.rt_exp2, 1)
                def iteration(li):
                    it = li + layer * ITERS
                    act.wait_ge(s.pt_ps, it + 1)
                    A_(gsr[0:C, :], ps[0:C, 4, GCOL:GCOL + EG], ACT.Copy)
                    A_(pmT[0:C, :], ps[0:C, 4, 0:T], ACT.Copy).then_inc(s.pt_done, 1)
                    for e in range(EG):
                        act.wait_ge(s.gu_ps, it * EG + e + 1)
                        if e >= 2:
                            act.wait_ge(s.act_done, it * EG + e - 1)
                        A_(sg[:, e % 2], ps[:, 2 + e % 2, 0:FT * C].rearrange("p (f c) -> p f c", f=FT),
                           ACT.Silu).then_inc(s.silu_done, 1)
                        if e == 0:
                            act.wait_ge(s.gs_ps, it + 1)
                            for hf in range(2):
                                A_(gs[:, 4 * hf:4 * hf + 4, :], ps[:, 6 + hf, 0:4 * C].rearrange("p (e c) -> p e c", e=4),
                                   ACT.Copy).then_inc(s.gs_done, 1)
                    act.wait_ge(s.dn_used, (it + 1) * EG)
                    for hf in range(2):
                        A_(ysb[0:C, 512 * hf:512 * (hf + 1)], ps[0:C, 4 + hf, :], ACT.Copy).then_inc(s.ysb_done, 1)

                with act.Fori(0, NG) as li:
                    iteration(li)
                with act.If(more(act, layer) > 0):
                    with act.Fori(NG, ITERS) as li:
                        iteration(li)
                with act.Else():
                    skip_rounds(act, layer, (s.gs_done, 2), (s.pt_done, 1), (s.silu_done, EG), (s.ysb_done, 2))
            moe(0, 1)
            norm_stats(2)
            act.dma_start(wsn[:, :, :], t["gm_spatial_w"][0].rearrange("h t s -> t h s")).then_inc(s.ws_loaded, 16)
            act.dma_start(bsr[0:1, :, 0:P], t["gm_spatial_b"]).then_inc(s.ws_loaded, 16)
            act.dma_start(lnw, t["gm_ln_w"][0:1, :].partition_broadcast(P)).then_inc(s.ws_loaded, 16)
            act.dma_start(lnb, t["gm_ln_b"][0:1, :].partition_broadcast(P)).then_inc(s.ws_loaded, 16)
            for c in range(NU + 2):
                if c < NU:
                    act.wait_ge(s.gm_v_ps, v_chan(c))
                    A_(vg[:, c % 4, :], ps[:, c % 4, 0:T], ACT.Gelu).then_inc(s.gm_v, 1)
                if c >= 2:
                    act.wait_ge(s.gm_v_ps, v_rows(c - 2))
                    for i, (r0, m) in enumerate(TOK):
                        last = A_(vrow[0:m, i, P * (c - 2):P * (c - 1)], ps[0:m, 4 + c % 2, P * i:P * (i + 1)], ACT.Copy,
                                  accum_out=lsum[0:m, NU * i + c - 2:NU * i + c - 1])
                    last.then_inc(s.gm_v, 1)
            for c in range(NU):
                if c >= 1 and c <= 3:
                    i, m = c - 1, TOK[c - 1][1]
                    act.wait_ge(s.gm_sum, i + 1)
                    if i:
                        act.wait_ge(s.gm_sq, i)
                    A_(sqj[0:m, :], vrow[0:m, i, :], ACT.Square, accum_out=lss[0:m, i:i + 1]).then_inc(s.gm_sq, 1)
                if c == 3:
                    act.wait_ge(s.gm_sq, 3)
                    A_(lrs, lss, ACT.Sqrt, scale=1.0 / DC, bias=epsb).then_inc(s.gm_rms, 1)
                act.wait_ge(s.gm_u_ps, c + 1)
                A_(uT[:, c, :], ps[:, c % 4, 0:T], ACT.Gelu).then_inc(s.gm_u, 1)
            for dt in range(8):
                act.wait_ge(s.gm_m_ps, NU + dt + 1)
                A_(hT[:, dt, :], ps[:, dt, 0:T], ACT.Copy).then_inc(s.gm_u, 1)
            act.wait_ge(s.gm_vn, 3)
            act.dma_start(t["chunk_v"][0].rearrange("b l c -> (b l) c"), vrow[0:TS, 2, :]).then_inc(s.out_misc, 16)
            act.dma_start(nfw, t["norm_final"].rearrange("(o d) -> o d", o=1).partition_broadcast(P))\
                .then_inc(s.nf_loaded, 16)
            moe(1, 3)
            norm_stats(4)

        @block.vector
        def _(dve):
            V = nc.vector
            n = [0]

            def ch(ins):
                n[0] += 1
                ins.then_inc(s.dve_chain, 1)
                dve.wait_ge(s.dve_chain, n[0])

            def norm(n_):
                dve.wait_ge(s.rms_done, n_ + 1)
                ch(V.reciprocal(rr[:, 3 * n_:3 * n_ + 3], rms[:, 3 * n_:3 * n_ + 3]))
                for i, (r0, m) in enumerate(TOK):
                    V.tensor_scalar(htok[0:m, i, :], x[0:m, i, :], rr[0:m, 3 * n_ + i:3 * n_ + i + 1], None,
                                    ALU.mult).then_inc(s.h_ready, 1)
                if n_:
                    dve.wait_ge(s.rest_loaded, 16 * REST)
                for k in range(KD):
                    dve.wait_ge(s.hT_ps, KD * n_ + k + 1)
                    V.tensor_scalar(hT[:, k, :], ps[:, k % 4, 0:T], nw[:, n_, k:k + 1], None,
                                    ALU.mult).then_inc(s.hT_done, 1)

            V.memset(cwc[:, 0:1], 0.0).then_inc(s.xadd, XADD0)
            V.memset(sm[:, 0:46], 1.0).then_inc(s.kpage_free, 4)
            dve.wait_ge(s.kpage_free, 4)
            ch(V.memset(htok[:, 2, :], 0.0))
            ch(V.memset(epsb, EPS))
            ch(V.memset(epsq, EPS * DB))
            ch(V.memset(fz, 0.0))
            ch(V.memset(lss, 1.0))
            ch(V.memset(gcc[:, 2, :], 0.0))
            ch(V.memset(kdc[:, 2, :], 0.0))
            V.memset(sm[:, 58:62], 0.0).then_inc(s.fz_sig, 1)
            dve.wait_ge(s.small_loaded, 16 * SMALL)
            norm(0)
            dve.wait_ge(s.fz_ps, 1)
            for i, (r0, m) in enumerate(TOK):
                V.tensor_copy(fz3[0:m, i, :], ps[0:m, 4, 16 * i:16 * i + 16]).then_inc(s.fz_copied, 1)
            dve.wait_ge(s.fz_copied, 3)
            ch(V.tensor_tensor(fz3, fz3, bc(biasrow.rearrange("p (o c) -> p o c", o=1), [P, 3, 16]), ALU.add))
            ch(V.tensor_scalar(fb, fz, -1.0, None, ALU.mult))
            V.tensor_tensor(fa, fz, fb, ALU.max).then_inc(s.fz_abs, 1)
            for c in range(NCT):
                last = V.memset(xc[:, c, 0:3], 0.0)
            ch(last)
            dve.wait_ge(s.fz_ln, 1)
            fb3 = fb.rearrange("p (t c) -> p t c", t=3)
            ch(V.scalar_tensor_tensor(lf, fz3[:, :, 0:8], 0.0, fb3[:, :, 0:8], ALU.min, ALU.subtract))
            ch(V.tensor_scalar(nlf, lf, -1.0, None, ALU.mult))
            ch(V.scalar_tensor_tensor(gg, fz3[:, :, 8:12], 0.0, fb3[:, :, 8:12], ALU.max, ALU.add))
            ch(V.scalar_tensor_tensor(gg, gg, -1.0, bc(expa.rearrange("p (o c) -> p o c", o=1), [P, 3, 4]),
                                      ALU.mult, ALU.mult))
            ch(V.tensor_scalar(beta, fz1.rearrange("p (t c) -> p t c", t=3)[:, :, 0:4], 1.0, None, ALU.add))
            ch(V.reciprocal(beta, beta))
            V.tensor_copy(lfn[0:TS, :].rearrange("p (b h q) -> p b h q", b=4, h=HA),
                          bc(nlf[0:TS, 2, :].rearrange("p (b h q) -> p b h q", b=1, q=1), [TS, 4, HA, QS]))\
                .then_inc(s.neglogf, 1)
            dve.wait_ge(s.cw_ps, 1)
            V.tensor_copy(cwc, ps[:, 6, 0:48]).then_inc(s.cw_done, 1)
            dve.wait_ge(s.cs_ps, 1)
            for c in range(NCT):
                last = V.tensor_copy(xc[:, c, XS:XC].rearrange("p (b w) -> p b w", b=NB)[:, :, 0:3],
                                     ps[:, 5, 24 * c:24 * c + 24].rearrange("p (b w) -> p b w", b=NB))
            last.then_inc(s.cs_copied, 1)
            dve.wait_ge(s.cw_done, 1)
            dve.wait_ge(s.cs_copied, 1)
            W_ = XC - 3
            for c in range(NCT):
                dve.wait_ge(s.proj_done, c + 1)
                for w in range(CW):
                    sc = cwc[:, w * NCT + c:w * NCT + c + 1]
                    src = xc[:, c, w:w + W_]
                    if w == 0:
                        ch(V.tensor_scalar(craw[:, c, 0:W_], src, sc, None, ALU.mult))
                    elif w < CW - 1:
                        ch(V.scalar_tensor_tensor(craw[:, c, 0:W_], src, sc, craw[:, c, 0:W_], ALU.mult, ALU.add))
                    else:
                        V.scalar_tensor_tensor(craw[:, c, 0:W_], src, sc, craw[:, c, 0:W_], ALU.mult, ALU.add)\
                            .then_inc(s.conv_raw, 1)
            ch(V.memset(qz[:, :, :], 0.0))
            dve.wait_ge(s.proj_done, 20)
            for b in range(NB):
                for c in range(NPAIR):
                    for e in range(2):
                        o = 32 * (b % 4) + 8 * c + 4 * e
                        last = V.tensor_copy(qz[64 * e:64 * e + 64, NPAIR * b + c, o:o + QS],
                                             qkT[64 * e:64 * e + 64, c, TP + QS * b:TP + QS * (b + 1)])
            ch(last)
            for j in range(6):
                i, (r0, m) = j // 2, TOK[j // 2]
                dve.wait_ge(s.kv_ps, j + 1)
                V.tensor_copy((ktok if j % 2 == 0 else vtok)[0:m, i, :], ps[0:m, j % 3, :]).then_inc(s.kv_copied, 1)
            dve.wait_ge(s.neglogf, 1)
            for h in range(HA + 1):
                if h < HA:
                    dve.wait_ge(s.pa_s_ps, h + 1)
                    for qb, c0, nk in ((0, 0, P), (1, P, TP)):
                        j = 2 * h + qb
                        V.tensor_reduce(pmax[:, j:j + 1], ps[:, h % 2, c0:c0 + nk], AX.X, ALU.max, negate=True)\
                            .then_inc(s.pa_max, 1)
                    for qb, c0, nk in ((0, 0, P), (1, P, TP)):
                        j = 2 * h + qb
                        dve.wait_ge(s.pa_exp, j + 1)
                        ch(V.reciprocal(pinv[:, j:j + 1], psm[:, j:j + 1]))
                        V.tensor_scalar(pP[:, h % 2, c0:c0 + nk], pP[:, h % 2, c0:c0 + nk], pinv[:, j:j + 1], None,
                                        ALU.mult).then_inc(s.pa_p, 1)
                if h:
                    g, o = h - 1, 64 * ((h - 1) % 2)
                    dve.wait_ge(s.pa_o_ps, h)
                    V.tensor_copy(mixT[o:o + 64, g // 2, 0:TP], ps[o:o + 64, 4 + g % 2, 0:TP]).then_inc(s.pa_o, 1)
                    if h == 1:
                        dve.wait_ge(s.cst_ps, 1)
                        V.tensor_copy(cst[0:27, :], ps[0:27, 5:8, :].rearrange("p a b -> p (a b)")).then_inc(s.cst_done, 1)
            for g in range(2):
                last = V.tensor_copy(eg[0:TS, g, :].rearrange("p (b h q) -> p b h q", b=4, h=HA),
                                     bc(ident[0:TS, 16 * g:16 * g + 16].rearrange("p (b h q) -> p b h q", h=1, q=QS),
                                        [TS, 4, HA, QS]))
            last.then_inc(s.qz_ready, 1)
            dve.wait_ge(s.bias_pages, 16 * 64)
            ch(V.tensor_scalar(lfp[:, :, :, :], lfp[:, :, :, :], -1.0, None, ALU.mult))
            for pg in range(NPAGE):
                dst, src = acc[:, :, 32 * pg:32 * pg + 32], lfp[:, :, pg, :]
                if pg == 0:
                    last = V.tensor_copy(dst, src)
                else:
                    last = V.tensor_tensor(dst, src, acc[:, :, 32 * pg - 32:32 * pg], ALU.add)
                ch(last)

            def spread(grp):
                for dst, src in ((lfx, lfp[:, grp].rearrange("p n b -> p (n b)")), (acx, acc[:, grp, :])):
                    last = V.tensor_copy(dst.rearrange("p n (b q) -> p (n b) q", q=QS),
                                         bc(src.rearrange("p (b q) -> p b q", q=1), [P, NPAGE * 32, QS]))
                last.then_inc(s.ks_done, 1)

            spread(0)
            for j in range(8):
                dve.wait_ge(s.dl_rms, j + 1)
                ch(V.reciprocal(dsq[:, j, :], dsq[:, j, :]))
                V.tensor_tensor(cv[:, j, :], cv[:, j, :], dsq[:, j, :], ALU.mult).then_inc(s.dl_qk, 1)
            for grp in range(2):
                dve.wait_ge(s.sa_s_ps, grp + 1)
                V.tensor_reduce(pmax[:, 16 + grp:17 + grp], ps[:, 0:3, :].rearrange("p a b -> p (a b)")[:, 0:1056],
                                AX.X, ALU.max, negate=True).then_inc(s.sa_max, 1)
                dve.wait_ge(s.sa_exp, grp + 1)
                ch(V.reciprocal(pinv[:, 16 + grp:17 + grp], psm[:, 16 + grp:17 + grp]))
                V.tensor_scalar(sS, sS, pinv[:, 16 + grp:17 + grp], None, ALU.mult).then_inc(s.sa_p, 1)
                dve.wait_ge(s.sa_o_ps, 2 * grp + 1)
                V.tensor_copy(sO, ps[:, 7, :]).then_inc(s.sa_o, 1)
                dve.wait_ge(s.sa_o_ps, 2 * grp + 2)
                for e in range(2):
                    dst = mixT[64 * e:64 * e + 64, 0:NPAIR, TP + 16 * grp:TP + 16 * grp + 16]\
                        .rearrange("p c (b q) -> p c b q", b=4)
                    for c in range(NPAIR):
                        src = ps[64 * e:64 * e + 64, 5, P * c:P * (c + 1)].rearrange("p (b j) -> p b j", b=4)
                        last = V.tensor_copy(dst[:, c], src[:, :, 8 * c + 4 * e:8 * c + 4 * e + 4])
                    last.then_inc(s.sa_o, 1)
                if grp == 0:
                    spread(1)
            dve.wait_ge(s.out_misc, 16 * 11)
            for j in range(6):
                i, (r0, m) = j // 2, TOK[j // 2]
                dve.wait_ge(s.dl_tok_ps, j + 1)
                V.tensor_copy((ktok if j % 2 == 0 else vtok)[0:m, i, :], ps[0:m, j % 3, :]).then_inc(s.dl_tok, 1)
            dve.wait_ge(s.dl_cols_ps, 1)
            for i in range(3):
                m = TOK[i][1]
                ch(V.tensor_copy(gcc[0:m, i, :], ps[0:m, 6, 4 * i:4 * i + 4]))
                last = V.tensor_tensor(kdc[0:m, i, :], ps[0:m, 6, 16 + 4 * i:20 + 4 * i], gcc[0:m, i, :], ALU.subtract)
            last.then_inc(s.dl_cols, 1)
            dve.wait_ge(s.dl_eR, 3)
            for i in range(3):
                m = TOK[i][1]
                for h in range(HB):
                    V.scalar_tensor_tensor(dDT[0:m, i, h, 0:m], ps[0:m, 3 + i, P * h:P * h + m], gcc[0:m, i, h:h + 1],
                                           negT[:, :] if i < 2 else negTS, ALU.subtract, ALU.add,
                                           ).then_inc(s.dl_dt, 1)
            for i in range(3):
                m = TOK[i][1]
                dve.wait_ge(s.dl_kk_ps, i + 1)
                dve.wait_ge(s.dl_dtx, i + 1)
                for w, dst in ((0, dLT), (1, dQK)):
                    src = ps[0:m, w, :].rearrange("p (h c) -> p h c", h=HB)[:, :, 0:m]
                    V.tensor_tensor(dst[0:m, i, :, 0:m], src, dDT[0:m, i, :, 0:m], ALU.mult).then_inc(s.dl_kk, 1)
            dve.wait_ge(s.dl_kk, 6)
            idb = bc(ident[:, :].rearrange("p (o c) -> p o c", o=1), [P, HB, P])
            for i in range(3):
                ch(V.tensor_copy(dT[:, i], idb))
                last = V.tensor_copy(dTT[:, i], idb)
            last.then_inc(s.dl_t, 1)
            dve.wait_ge(s.dl_t, 1)

            def inv_m(l):
                for i in inv_tiles(l):
                    m = TOK[i][1]
                    V.tensor_tensor(dMT[0:m, i, :, 0:m], dLT[0:m, i, :, 0:m],
                                    bc(lvl[0:m, l, 0:m].rearrange("p (o c) -> p o c", o=1), [m, HB, m]),
                                    ALU.mult).then_inc(s.dl_mt, 1)

            inv_m(0)
            for l in range(7):
                for i in inv_tiles(l):
                    m = TOK[i][1]
                    dve.wait_ge(s.dl_u_ps, inv_no(l, i))
                    V.tensor_tensor(dU[0:m, i, :, 0:m], inv_ps(i, 0),
                                    bc(beta[0:m, i, :].rearrange("p (h o) -> p h o", o=1), [m, HB, m]),
                                    ALU.mult).then_inc(s.dl_u, 1)
                if l < 6:
                    inv_m(l + 1)
                for i in inv_tiles(l):
                    m = TOK[i][1]
                    dve.wait_ge(s.dl_t_ps, inv_no(l, i))
                    V.tensor_tensor(dT[0:m, i, :, 0:m], dT[0:m, i, :, 0:m], inv_ps(i, 1), ALU.subtract)\
                        .then_inc(s.dl_t, 1)
                    V.tensor_tensor(dTT[0:m, i, :, 0:m], dTT[0:m, i, :, 0:m], inv_ps(i, 2), ALU.subtract)\
                        .then_inc(s.dl_t, 1)
            dve.wait_ge(s.dl_t, 1 + 2 * inv_no(6, 1))
            dve.wait_ge(s.dl_cols, 2)
            ch(V.tensor_tensor(bex, beta, egc, ALU.mult))
            for i in range(3):
                m = TOK[i][1]
                cb = lambda a: bc(a[0:m, i, :].rearrange("p (h o) -> p h o", o=1), [m, HB, P])
                V.tensor_tensor(vb[0:m, i], vdt[0:m, i], cb(beta), ALU.mult)
                ch(V.tensor_tensor(kbe[0:m, i], kdt[0:m, i], cb(bex), ALU.mult))
                last = V.tensor_tensor(kdt[0:m, i], kdt[0:m, i], cb(kdc), ALU.mult)
            last.then_inc(s.dl_scaled, 2)
            dve.wait_ge(s.dl_eR, 3)
            for i, (r0, m) in enumerate(TOK):
                last = V.tensor_tensor(cv[:, 0:HB, r0:r0 + m], cv[:, 0:HB, r0:r0 + m], eR[:, i, :, 0:m], ALU.mult)
            last.then_inc(s.dl_qdec, 1)
            for i in range(3):
                m = TOK[i][1]
                dve.wait_ge(s.dl_w_ps, i + 1)
                V.tensor_copy(wv[0:m, i], ps[0:m, 0, :].rearrange("p (h c) -> p h c", h=HB)).then_inc(s.dl_w, 1)
                V.tensor_copy(wkT[:, i, :, 0:m], ps[:, 1, :].rearrange("p (h c) -> p h c", h=HB)[:, :, 0:m])\
                    .then_inc(s.dl_w, 1)
            hv = lambda b: ps[:, b, :].rearrange("p (h c) -> p h c", h=HB)
            dve.wait_ge(s.dl_s_ps, 1)
            V.tensor_copy(Sp[:, 0], hv(2)).then_inc(s.dl_s, 1)
            dve.wait_ge(s.dl_v1_ps, 1)
            V.tensor_tensor(wv[:, 1], wv[:, 1], hv(3), ALU.subtract).then_inc(s.dl_v1, 1)
            ch(V.tensor_tensor(Sp[:, 1], Sp[:, 0], bc(eR[:, 1, :, P - 1:P], [P, HB, P]), ALU.mult))
            dve.wait_ge(s.dl_s_ps, 2)
            V.tensor_tensor(Sp[:, 1], Sp[:, 1], hv(2), ALU.add).then_inc(s.dl_st_out, 1)
            dve.wait_ge(s.dl_vs_ps, 1)
            V.tensor_copy(vsT, ps[:, 4, 0:HB * TS]).then_inc(s.dl_vsT, 1)
            dve.wait_ge(s.dl_vt_ps, 1)
            V.tensor_tensor(wv[0:TS, 2], wv[0:TS, 2], ps[0:TS, 5, :].rearrange("p (h c) -> p h c", h=HB),
                            ALU.subtract).then_inc(s.dl_vs, 1)
            dve.wait_ge(s.dl_vs, 1)
            for b in range(NB):
                V.tensor_scalar(vexp[0:TS, b, :], wv[0:TS, 2].rearrange("p h e -> p (h e)"), bsel[:, b:b + 1], None,
                                ALU.mult).then_inc(s.dl_vexp, 1)
            dve.wait_ge(s.dl_o_ps, HB)
            S04 = S0.rearrange("p (b h) e -> p b h e", h=HB)
            for h in range(HB):
                last = V.tensor_tensor(S04[:, :, h, :], S04[:, :, h, :],
                                       bc(eR[:, 2, h, QS - 1:TS:QS].rearrange("p (b o) -> p b o", o=1), [P, NB, P]),
                                       ALU.mult)
            ch(last)
            dve.wait_ge(s.dl_orms, HB)
            ch(V.reciprocal(osq, osq))
            ch(V.tensor_tensor(oT, oT, osq, ALU.mult))
            for h in range(HB):
                V.scalar_tensor_tensor(mixT[:, 4 + h, :], oT[:, h, :], onw, gT[:, h, :], ALU.mult,
                                       ALU.mult).then_inc(s.dl_mixed, 1)
            for j in range(8):
                h, q = j // 2, j % 2
                dve.wait_ge(s.dl_su_ps, j + 1)
                V.tensor_tensor(S04[:, 4 * q:4 * q + 4, h, :], S04[:, 4 * q:4 * q + 4, h, :],
                                ps[:, 6 + j % 2, :].rearrange("p (b e) -> p b e", b=4), ALU.add).then_inc(s.dl_su, 1)

            def add_out(used):
                dve.wait_ge(s.w_used, used)
                for i, (r0, m) in enumerate(TOK):
                    for hf in range(2):
                        last = V.tensor_tensor(x[0:m, i, 512 * hf:512 * (hf + 1)], x[0:m, i, 512 * hf:512 * (hf + 1)],
                                               ps[0:m, 2 * i + hf, :], ALU.add)
                    last.then_inc(s.x_new, 1)

            add_out(4)

            def first_of(dst, eq, width, base):
                rv = bc(rev[:, NE - width:NE].rearrange("p (o c) -> p o c", o=1), [P, 3, width])
                ch(V.tensor_tensor(eq, eq, rv, ALU.mult))
                ch(V.tensor_reduce(mr, eq, AX.X, ALU.max))
                ch(V.tensor_tensor(dst, eq, bc(mr, [P, 3, width]), ALU.is_equal))

            def moe(layer, n_):
                norm(n_)
                dve.wait_ge(s.rl_ps, layer + 1)
                dve.wait_ge(s.out_misc, 16 * 13)
                ch(V.memset(lg, 0.0))
                for i, (r0, m) in enumerate(TOK):
                    ch(V.tensor_copy(lg[0:m, i, :], ps[0:m, 4, 36 * i:36 * i + 36]))
                ch(V.tensor_reduce(m4, lg[:, :, 0:NG], AX.X, ALU.max))
                V.tensor_tensor(d4, lg[:, :, 0:NG], bc(m4, [P, 3, NG]), ALU.subtract).then_inc(s.rt_e4x, 1)
                dve.wait_ge(s.rt_e4x, 2 * layer + 1)
                ch(V.tensor_scalar(eq4, d4, 0.0, None, ALU.is_ge))
                dve.wait_ge(s.rt_exp2, 2 * layer + 1)
                ch(V.tensor_reduce(s4, e4, AX.X, ALU.add))
                first_of(oh4, eq4, NG, 0)
                ch(V.tensor_scalar(pen, oh4, BIG, -BIG, ALU.mult, ALU.add))
                for g in range(NG):
                    last = V.tensor_tensor(lem[:, :, EG * g:EG * (g + 1)], lg[:, :, NG + EG * g:NG + EG * (g + 1)],
                                           bc(pen[:, :, g:g + 1], [P, 3, EG]), ALU.add)
                last.then_inc(s.rt_oh, 1)
                dve.wait_ge(s.rt_oh, layer + 1)
                ch(V.tensor_reduce(v1, lem, AX.X, ALU.max))
                ch(V.tensor_tensor(eqa, lem, bc(v1, [P, 3, NE]), ALU.is_equal))
                first_of(oh1, eqa, NE, 0)
                ch(V.scalar_tensor_tensor(lem, oh1, -2.0 * BIG, lem, ALU.mult, ALU.add))
                ch(V.tensor_reduce(v2, lem, AX.X, ALU.max))
                ch(V.tensor_tensor(eqa, lem, bc(v2, [P, 3, NE]), ALU.is_equal))
                first_of(oh2, eqa, NE, 0)
                V.tensor_tensor(ex2, v2, v1, ALU.subtract).then_inc(s.rt_e4x, 1)
                dve.wait_ge(s.rank_ps, layer + 1)
                ch(V.tensor_reduce(gmax, ps[0:1, 5, 16:20], AX.X, ALU.max))
                V.tensor_scalar(flag[:, layer:layer + 1], gmax, float(C), None, ALU.is_gt).then_inc(s.flag_ready, 1)
                ch(V.memset(rk, 0.0))
                for i, (r0, m) in enumerate(TOK):
                    ch(V.tensor_copy(rk[0:m, i, :], ps[0:m, 5, 4 * i:4 * i + 4]))
                ch(V.tensor_scalar(rk2, rk, float(C), float((NG - 1) * C), ALU.is_gt, ALU.mult))
                ch(V.tensor_scalar(eq4, rk, float(2 * C), float((NG - 1) * C), ALU.is_gt, ALU.mult))
                ch(V.tensor_tensor(rk, rk, rk2, ALU.add))
                ch(V.tensor_tensor(rk, rk, eq4, ALU.add))
                for g in range(NG):
                    last = V.tensor_scalar(rk[:, :, g:g + 1], rk[:, :, g:g + 1], float(C * g - 1), None, ALU.add)
                ch(last)
                ch(V.tensor_tensor(rk, rk, oh4, ALU.mult))
                ch(V.tensor_reduce(pos, rk, AX.X, ALU.add))
                ch(V.memset(pm[:, 2, :], 0.0))
                ch(V.tensor_copy(iota[:, 1, :], iota[:, 0, :]))

                def permutation():
                    for i, (r0, m) in enumerate(TOK):
                        V.tensor_scalar(pm[0:m, i, :], iota[0:m, 1, :], pos[0:m, i, :], None,
                                        ALU.is_equal).then_inc(s.perm_ready, 1)

                permutation()
                dve.wait_ge(s.rt_exp2, 2 * layer + 2)
                ch(V.tensor_scalar(w1, ex2, 1.0, None, ALU.add))
                ch(V.tensor_tensor(w1, w1, s4, ALU.mult))
                ch(V.reciprocal(w1, w1))
                ch(V.tensor_tensor(w2, w1, ex2, ALU.mult))
                ch(V.tensor_tensor(oh1, oh1, bc(w1, [P, 3, NE]), ALU.mult))
                ch(V.tensor_tensor(oh2, oh2, bc(w2, [P, 3, NE]), ALU.mult))
                ch(V.tensor_tensor(oh1, oh1, oh2, ALU.add))
                ch(V.tensor_tensor(oh2[:, :, 0:16], oh1[:, :, 0:16], oh1[:, :, 16:32], ALU.add))
                V.tensor_tensor(g8, oh2[:, :, 0:8], oh2[:, :, 8:16], ALU.add).then_inc(s.rank_done, 1)

                def iteration(li):
                    it = li + layer * ITERS
                    dve.wait_ge(s.hg_ps, it + 1)
                    for k in range(2):
                        V.tensor_tensor(hg[:, 4 * k:4 * k + 4, :], ps[:, k, 0:4 * C].rearrange("p (k c) -> p k c", k=4),
                                        bc(nw[:, n_, 4 * k:4 * k + 4].rearrange("p (k o) -> p k o", o=1), [P, 4, C]),
                                        ALU.mult).then_inc(s.hg_done, 1)
                    dve.wait_ge(s.pt_done, it + 1)
                    V.tensor_tensor(dg[0:C], bc(ident[0:C, 0:C].rearrange("p (o c) -> p o c", o=1), [C, EG, C]),
                                    bc(gsr[0:C, :].rearrange("p (e o) -> p e o", o=1), [C, EG, C]),
                                    ALU.mult).then_inc(s.moe_chain, 1)
                    for e in range(EG):
                        dve.wait_ge(s.silu_done, it * EG + e + 1)
                        V.tensor_tensor(a1[:, e % 2], ps[:, 2 + e % 2, FT * C:2 * FT * C]
                                        .rearrange("p (f c) -> p f c", f=FT), sg[:, e % 2], ALU.mult)\
                            .then_inc(s.moe_chain, 1)
                        dve.wait_ge(s.moe_chain, it * (EG + 2) + e + 2)
                        if e == 0:
                            dve.wait_ge(s.gs_done, 2 * it + 2)
                        if e >= 2:
                            dve.wait_ge(s.dn_used, it * EG + e - 1)
                        V.tensor_tensor(av[:, e % 2], a1[:, e % 2],
                                        bc(gs[:, e, :].rearrange("p (o c) -> p o c", o=1), [P, FT, C]),
                                        ALU.mult).then_inc(s.act_done, 1)
                    V.tensor_scalar(iota[:, 1, :], iota[:, 1, :], float(C), None, ALU.add).then_inc(s.moe_chain, 1)
                    dve.wait_ge(s.moe_chain, it * (EG + 2) + EG + 2)
                    dve.wait_ge(s.pt_ps, it + 1)
                    permutation()
                    for j in range(6):
                        i, (r0, m) = j // 2, TOK[j // 2]
                        xs = x[0:m, i, 512 * (j % 2):512 * (j % 2 + 1)]
                        dve.wait_ge(s.sc_ps, it * 6 + j + 1)
                        V.tensor_tensor(xs, xs, ps[0:m, (6, 7, 0, 1)[j % 4], :], ALU.add).then_inc(s.xadd, 1)
                    dve.wait_ge(s.xadd, XADD0 + it * 6 + 6)

                with dve.Fori(0, NG) as li:
                    iteration(li)
                with dve.If(more(dve, layer) > 0):
                    with dve.Fori(NG, ITERS) as li:
                        iteration(li)
                with dve.Else():
                    skip_rounds(dve, layer, (s.perm_ready, 3), (s.hg_done, 2), (s.moe_chain, EG + 2), (s.act_done, EG), (s.xadd, 6))
                V.memset(cwc[:, 0:1], 0.0).then_inc(s.x_new, 3)

            moe(0, 1)
            norm(2)
            for h in range(HC):
                dve.wait_ge(s.ws_ps, 4 * (h // 4 + 1))
                V.tensor_tensor(wmT[:, h, :], ps[:, 6, P * (h % 4):P * (h % 4 + 1)], ut, ALU.mult).then_inc(s.ws_done, 1)
            V.tensor_copy(rep[0:QS], bc(ident[0:QS, 0:QS].rearrange("p (o q) -> p o q", o=1), [QS, NB, QS]))\
                .then_inc(s.ws_done, 1)
            dve.wait_ge(s.ws_loaded, 64)
            ch(V.tensor_copy(bsr[0:1, :, P:TP], bsr[0:1, :, 0:P]))
            for b in range(NB):
                last = V.tensor_copy(bsr[0:1, :, TP + QS * b:TP + QS * (b + 1)], bsr[0:1, :, 0:QS])
            last.then_inc(s.gm_bias, 1)
            dve.wait_ge(s.wrep_ps, 1)
            ch(V.tensor_copy(wrep[0:TS, :], ps[0:TS, 7, 0:HC * QS]))
            for h in range(HC):
                V.tensor_tensor(wS[0:TS, h, :].rearrange("p (b q) -> p b q", b=NB),
                                bc(wrep[0:TS, QS * h:QS * (h + 1)].rearrange("p (o q) -> p o q", o=1), [TS, NB, QS]),
                                same.rearrange("p (b q) -> p b q", b=NB), ALU.mult).then_inc(s.wrep_done, 1)
            dve.wait_ge(s.gm_v, 2 * NU)
            for i, (r0, m) in enumerate(TOK):
                ch(V.tensor_reduce(lmu[0:m, i:i + 1], lsum[0:m, NU * i:NU * (i + 1)], AX.X, ALU.add))
                ch(V.tensor_scalar(lmu[0:m, i:i + 1], lmu[0:m, i:i + 1], 1.0 / DC, None, ALU.mult))
                V.tensor_scalar(vrow[0:m, i, :], vrow[0:m, i, :], lmu[0:m, i:i + 1], None,
                                ALU.subtract).then_inc(s.gm_sum, 1)
            dve.wait_ge(s.gm_rms, 1)
            ch(V.reciprocal(lrs, lrs))
            for i, (r0, m) in enumerate(TOK):
                ch(V.scalar_tensor_tensor(vrow[0:m, i, :], vrow[0:m, i, :], lrs[0:m, i:i + 1], lnw[0:m, :],
                                          ALU.mult, ALU.mult))
                V.tensor_tensor(vrow[0:m, i, :], vrow[0:m, i, :], lnb[0:m, :], ALU.add).then_inc(s.gm_vn, 1)
            dve.wait_ge(s.gm_u, NU)
            for c in range(NU):
                dve.wait_ge(s.gm_m_ps, c + 1)
                V.tensor_tensor(uT[:, c, :], uT[:, c, :], ps[:, c % 4, 0:T], ALU.mult).then_inc(s.gm_m, 1)
            for dt in range(8):
                dve.wait_ge(s.gm_m_ps, NU + 8 + dt + 1)
                xs = x[:, 0:2, P * dt:P * (dt + 1)]
                V.tensor_tensor(xs, xs, ps[:, dt, 0:TP].rearrange("p (i c) -> p i c", i=2), ALU.add)
                xs = x[0:TS, 2, P * dt:P * (dt + 1)]
                last = V.tensor_tensor(xs, xs, ps[0:TS, dt, TP:TP + P], ALU.add)
            last.then_inc(s.x_new, 3)
            moe(1, 3)
            dve.wait_ge(s.rms_done, 5)
            ch(V.reciprocal(rr[:, 12:15], rms[:, 12:15]))
            dve.wait_ge(s.nf_loaded, 16)
            for i, (r0, m) in enumerate(TOK):
                V.scalar_tensor_tensor(htok[0:m, i, :], x[0:m, i, :], rr[0:m, 12 + i:13 + i], nfw[0:m, :], ALU.mult,
                                       ALU.mult).then_inc(s.fin_y, 1)


OUTS = [("y_prompt", (1, TP, D)), ("y_sample", (NB, QS, D)), ("k_prompt", (1, 1, TP, HA, DA)),
        ("v_prompt", (1, 1, TP, HA, DA)), ("logf_prompt", (1, 1, TP, HA)), ("delta_prompt", (1, 1, HB, DB, DB)),
        ("conv_prompt", (1, 1, CW - 1, NCT * P)), ("k_sample", (1, NB, QS, HA, DA)), ("v_sample", (1, NB, QS, HA, DA)),
        ("logf_sample", (1, NB, QS, HA)), ("delta_sample", (1, NB, HB, DB, DB)),
        ("conv_sample", (1, NB, CW - 1, NCT * P)), ("chunk_v", (1, NB, QS, DC))]


def kernel(**inputs):
    import numpy as np
    import concourse.bacc as bacc
    from concourse.bass_utils import run_bass_kernel_spmd

    nc = bacc.Bacc("TRN2", target_bir_lowering=False, num_devices=1, dynamic_dma_scratch_size=2048)
    arrays, t = {}, {}
    for name, value in inputs.items():
        a = np.ascontiguousarray(value)
        arrays[f"in_{name}"] = a
        t[name] = nc.dram_tensor(f"in_{name}", a.shape, mybir.dt.from_np(a.dtype), kind="ExternalInput").ap()
    for name, shape in OUTS:
        t[name] = nc.dram_tensor(f"out_{name}", shape, F32, kind="ExternalOutput").ap()
    build(nc, t)
    r = run_bass_kernel_spmd(nc, [arrays], core_ids=[0])
    return tuple(r.results[0][f"out_{name}"] for name, _ in OUTS)
```
